# Optimizing a Trainium2 kernel written in Bass

```python
import jax, jax.numpy as jnp
from jax import lax
import numpy as np

D_MODEL = 2048
BATCH = 1
SEQ = 256
DEPTH = 1

CHUNK = 64
D_MIX = D_MODEL

HG_WIDTH = D_MIX // 2
HG_EXPAND = 128
HG_HEADS = HG_WIDTH // HG_EXPAND
HG_DK = HG_EXPAND
HG_DV = HG_WIDTH // HG_HEADS

MLA_WIDTH = D_MIX - HG_WIDTH
V_DIM = 128
MLA_HEADS = MLA_WIDTH // V_DIM
QK_NOPE = 128
QK_ROPE = 64
QK_DIM = QK_NOPE + QK_ROPE
Q_LORA = 512
KV_LORA = 512
ROPE_THETA = 10000.0
Q_BLOCK = 128
ATTN_SCALE = QK_DIM ** -0.5

D_FF = ((8 * D_MODEL // 3 + 255) // 256) * 256

NORM_EPS = 1e-6

IN_SIZES = (HG_WIDTH, HG_WIDTH, HG_WIDTH, HG_WIDTH, Q_LORA, KV_LORA, QK_ROPE)
D_IN = sum(IN_SIZES)
IN_SPLITS = tuple(int(v) for v in np.cumsum(IN_SIZES)[:-1])

kernel_name = "hymba_style_hgrn2_mla_swiglu"

def rms_norm(x, w):
    xf = x.astype(jnp.float32)
    y = xf * lax.rsqrt(jnp.mean(xf * xf, axis=-1, keepdims=True) + NORM_EPS)
    return (y * w.astype(jnp.float32)).astype(x.dtype)

def rope_tables(positions):
    inv_freq = 1.0 / (ROPE_THETA ** (jnp.arange(0, QK_ROPE, 2, dtype=jnp.float32) / QK_ROPE))
    ang = positions.astype(jnp.float32)[..., None] * inv_freq
    return jnp.cos(ang)[:, :, None, :], jnp.sin(ang)[:, :, None, :]

def rope_tail(t, cos, sin):
    t_nope, t_rope = jnp.split(t, [QK_NOPE], axis=-1)
    r1, r2 = jnp.split(t_rope, 2, axis=-1)
    c = cos.astype(t.dtype)
    s = sin.astype(t.dtype)
    return jnp.concatenate([t_nope, r1 * c - r2 * s, r1 * s + r2 * c], axis=-1)

def hgrn2_mixer(q, f_pre, i, g, lb, norm_w):
    B_, S_, _ = q.shape
    n_chunks = S_ // CHUNK
    qf = jax.nn.silu(q.astype(jnp.float32))
    f = lb + (1.0 - lb) * jax.nn.sigmoid(f_pre.astype(jnp.float32))
    kf = 1.0 - f

    def chunked(t, d):
        return t.reshape(B_, n_chunks, CHUNK, HG_HEADS, d).transpose(1, 0, 3, 2, 4)

    qc = chunked(qf, HG_DK)
    kc = chunked(kf, HG_DK)
    vc = chunked(i.astype(jnp.float32), HG_DV)
    bc = jnp.cumsum(chunked(jnp.log(f), HG_DK), axis=3)
    causal = jnp.tril(jnp.ones((CHUNK, CHUNK), dtype=bool))[:, :, None]

    def step(state, inp):
        q_c, k_c, v_c, b_c = inp
        rel = b_c[:, :, :, None, :] - b_c[:, :, None, :, :]
        decay = jnp.exp(jnp.where(causal, rel, -jnp.inf))
        scores = jnp.einsum('bhtd,bhsd,bhtsd->bhts', q_c, k_c, decay)
        o = (jnp.einsum('bhts,bhsv->bhtv', scores, v_c)
             + jnp.einsum('bhtd,bhdv->bhtv', q_c * jnp.exp(b_c), state))
        b_last = b_c[:, :, -1:, :]
        state = (jnp.exp(b_last[:, :, 0, :, None]) * state
                 + jnp.einsum('bhsd,bhsv->bhdv', k_c * jnp.exp(b_last - b_c), v_c))
        return state, o

    state0 = jnp.zeros((B_, HG_HEADS, HG_DK, HG_DV), jnp.float32)
    _, o = lax.scan(step, state0, (qc, kc, vc, bc))
    o = o.transpose(1, 0, 3, 2, 4).reshape(B_, S_, HG_HEADS, HG_DV)
    gate = jax.nn.silu(g.astype(jnp.float32)).reshape(B_, S_, HG_HEADS, HG_DV)
    o = rms_norm(o, norm_w) * gate
    return o.reshape(B_, S_, HG_WIDTH).astype(g.dtype)

def mla_mixer(c_q, c_kv, k_rope, cos, sin, q_norm_w, w_uq, kv_norm_w, w_ukv, q_head_w, k_head_w):
    B_, S_, _ = c_q.shape
    q = (rms_norm(c_q, q_norm_w) @ w_uq).reshape(B_, S_, MLA_HEADS, QK_DIM)
    kv = (rms_norm(c_kv, kv_norm_w) @ w_ukv).reshape(B_, S_, MLA_HEADS, QK_NOPE + V_DIM)
    k_nope, v = jnp.split(kv, [QK_NOPE], axis=-1)
    k = jnp.concatenate(
        [k_nope, jnp.broadcast_to(k_rope[:, :, None, :], (B_, S_, MLA_HEADS, QK_ROPE))], axis=-1)
    q = rope_tail(rms_norm(q, q_head_w), cos, sin)
    k = rope_tail(rms_norm(k, k_head_w), cos, sin)

    n_blocks = S_ // Q_BLOCK
    q_blocks = q.reshape(B_, n_blocks, Q_BLOCK, MLA_HEADS, QK_DIM).transpose(1, 0, 2, 3, 4)
    key_chunk = jnp.arange(S_) // CHUNK

    def attend(args):
        q_blk, blk = args
        query_chunk = (blk * Q_BLOCK + jnp.arange(Q_BLOCK)) // CHUNK
        s = jnp.einsum('bqhd,bkhd->bhqk', q_blk, k).astype(jnp.float32) * ATTN_SCALE
        s = jnp.where(key_chunk[None, :] <= query_chunk[:, None], s, -jnp.inf)
        p = jax.nn.softmax(s, axis=-1).astype(v.dtype)
        return jnp.einsum('bhqk,bkhv->bqhv', p, v)

    o = lax.map(attend, (q_blocks, jnp.arange(n_blocks)))
    return o.transpose(1, 0, 2, 3, 4).reshape(B_, S_, MLA_WIDTH)

def setup_inputs(seed: int = 0) -> dict:
    key = jax.random.key(seed)
    ks = jax.random.split(key, 17)
    f32 = jnp.float32

    def nrm(k, shape, fan_in):
        return jax.random.normal(k, shape, f32) * (fan_in ** -0.5)

    def gain(k, shape):
        return 1.0 + 0.02 * jax.random.normal(k, shape, f32)

    x = jax.random.normal(ks[0], (BATCH, SEQ, D_MODEL), f32)
    offset = jax.random.randint(ks[1], (BATCH, 1), 0, 4096, dtype=jnp.int32)
    positions = offset + jnp.arange(SEQ, dtype=jnp.int32)[None, :]
    return {
        "x": x,
        "positions": positions,
        "attn_norm_w": gain(ks[2], (DEPTH, D_MODEL)),
        "w_in": nrm(ks[3], (DEPTH, D_MODEL, D_IN), D_MODEL),
        "hgrn_lb": 0.5 * jax.random.normal(ks[4], (DEPTH + 1, HG_HEADS * HG_DK), f32),
        "hgrn_norm_w": gain(ks[5], (DEPTH, HG_DV)),
        "mla_q_norm_w": gain(ks[6], (DEPTH, Q_LORA)),
        "w_uq": nrm(ks[7], (DEPTH, Q_LORA, MLA_HEADS * QK_DIM), Q_LORA),
        "mla_kv_norm_w": gain(ks[8], (DEPTH, KV_LORA)),
        "w_ukv": nrm(ks[9], (DEPTH, KV_LORA, MLA_HEADS * (QK_NOPE + V_DIM)), KV_LORA),
        "q_head_norm_w": gain(ks[10], (DEPTH, QK_DIM)),
        "k_head_norm_w": gain(ks[11], (DEPTH, QK_DIM)),
        "w_out": nrm(ks[12], (DEPTH, D_MIX, D_MODEL), D_MIX),
        "ffn_norm_w": gain(ks[13], (DEPTH, D_MODEL)),
        "w_gate_up": nrm(ks[14], (DEPTH, D_MODEL, 2 * D_FF), D_MODEL),
        "w_down": nrm(ks[15], (DEPTH, D_FF, D_MODEL), D_FF),
    }

def reference(x, positions, attn_norm_w, w_in, hgrn_lb, hgrn_norm_w, mla_q_norm_w, w_uq,
              mla_kv_norm_w, w_ukv, q_head_norm_w, k_head_norm_w, w_out, ffn_norm_w,
              w_gate_up, w_down):
    cos, sin = rope_tables(positions)
    lower_bounds = jnp.cumsum(jax.nn.softmax(hgrn_lb.astype(jnp.float32), axis=0), axis=0)
    for layer in range(DEPTH):
        h = rms_norm(x, attn_norm_w[layer])
        proj = h @ w_in[layer]
        hq, hf, hi, hg, c_q, c_kv, k_r = jnp.split(proj, IN_SPLITS, axis=-1)
        o_a = hgrn2_mixer(hq, hf, hi, hg, lower_bounds[layer], hgrn_norm_w[layer])
        o_b = mla_mixer(c_q, c_kv, k_r, cos, sin, mla_q_norm_w[layer], w_uq[layer],
                        mla_kv_norm_w[layer], w_ukv[layer], q_head_norm_w[layer],
                        k_head_norm_w[layer])
        x = x + jnp.concatenate([o_a, o_b], axis=-1) @ w_out[layer]
        h = rms_norm(x, ffn_norm_w[layer])
        gate, up = jnp.split(h @ w_gate_up[layer], 2, axis=-1)
        x = x + (jax.nn.silu(gate) * up) @ w_down[layer]
    return x


_drawn_inputs = setup_inputs


def setup_inputs(seed=0):
    import zlib

    import numpy as np

    out = dict(_drawn_inputs(seed))
    spreads = {}
    factors = {'attn_norm_w': 4.244,
     'hgrn_norm_w': 5.691,
     'mla_q_norm_w': 8.0,
     'mla_kv_norm_w': 8.0,
     'q_head_norm_w': 8.0,
     'k_head_norm_w': 8.0,
     'ffn_norm_w': 11.998}
    for name, (base, spread) in spreads.items():
        noise = np.random.default_rng([zlib.crc32(name.encode()), seed]).standard_normal(out[name].shape)
        drawn = base * np.exp(spread * noise) if base else spread * noise
        out[name] = __import__('jax').numpy.asarray(drawn.astype(out[name].dtype))
    for name, factor in factors.items():
        out[name] = (out[name] * factor).astype(out[name].dtype)
    return out
```

```python
from contextlib import ExitStack

import numpy as np

import concourse.bass as bass
from concourse import mybir

F32 = mybir.dt.float32
F32R = mybir.dt.float32r
I32 = mybir.dt.int32
ALU = mybir.AluOpType
ACT = mybir.ActivationFunctionType
AX = mybir.AxisListType

P = 128
D = 2048
SEQ = 256
NT = SEQ // P
CHUNK = 64
KT = D // P
HG = 1024
GH = 4
GW = GH * P
LORA = 512
HEADS = 8
NOPE, ROPE = 128, 64
QK = NOPE + ROPE
HALF = ROPE // 2
D_FF = 5632
NB = 512
EPS = 1e-6
SCALE = float(QK) ** -0.5
MASKED = -1e30
LEVELS = 6
RING = 4
LEAD = 3
GRAN = 1024
SIDE = 4

V_ATTN, V_FFN, V_QN, V_KVN, V_HG, V_ROWS = 0, KT, 2 * KT, 2 * KT + 4, 2 * KT + 8, 2 * KT + 9


def main_blocks():
    def rows(n, first=0):
        return [first + P * k for k in range(n)]
    w = []
    w.append(("cq", 0, "w_in", 4 * HG, LORA, rows(KT), 2))
    w.append(("ckv", 0, "w_in", 4 * HG + LORA, LORA, rows(KT), 2))
    w.append(("kr", 0, "w_in", 4 * HG + 2 * LORA, ROPE, rows(KT), KT))
    w.append(("hq", 0, "w_in", 0, GW, rows(KT), 2))
    w.append(("hf", 0, "w_in", HG, GW, rows(KT), 2))
    w += [("uq", j, "w_uq", 2 * QK * j, 2 * QK, rows(LORA // P), 2) for j in range(HEADS // 2)]
    w += [("ukv", j, "w_ukv", NB * j, NB, rows(LORA // P), 2) for j in range(HEADS // 2)]
    w.append(("hi", 0, "w_in", 2 * HG, GW, rows(KT), 2))
    w.append(("hg", 0, "w_in", 3 * HG, GW, rows(KT), 2))
    for n, kind in enumerate(("hq", "hf", "hi", "hg")):
        w.append((kind, 1, "w_in", n * HG + GW, GW, rows(KT), 2))
    w += [("out1", c, "w_out", NB * c, NB, rows(8, HG) + rows(4), 2) for c in range(4)]
    w += [("out2", c, "w_out", NB * c, NB, rows(4, GW), 2) for c in range(4)]
    return w


BLOCKS = main_blocks()
GRANULES = [(b, k, blk[6]) for b, blk in enumerate(BLOCKS) for k in range(0, len(blk[5]), blk[6])]
G0 = len(GRANULES)
END = {blk[:2]: 1 + max(g for g, x in enumerate(GRANULES) if x[0] == b) for b, blk in enumerate(BLOCKS)}
BLOCK_OF = {blk[:2]: b for b, blk in enumerate(BLOCKS)}
NFF = D_FF // NB
GU = 2 * KT // 2
DOWN_KT = D_FF // P
DN = DOWN_KT // 2
G1 = G0 + NFF * GU


def schedule():
    s = [(-1, ("vec",))] + [(-1, ("x", j)) for j in range(4)]
    s += [(j - 4, ("x", j)) for j in range(4, 8)]
    s += [(4, ("r1a",)), (5, ("r1b",)), (6, ("angles",)), (7, ("sines",))]
    e = END[("cq", 0)]
    s += [(e, ("lat_a", 0)), (e + 1, ("lat_b", 0)), (e + 4, ("lat_t", 0, 0)), (e + 4, ("lat_t", 0, 1))]
    s += [(e + 5, ("lb_a", 0)), (e + 6, ("lb_b", 0))]
    e = END[("ckv", 0)]
    s += [(e, ("lat_a", 1)), (e + 1, ("lat_b", 1)), (e + 5, ("lat_t", 1, 0)), (e + 5, ("lat_t", 1, 1))]
    s += [(e + 1, ("kr_a",)), (e + 2, ("kr_b",))]
    for j in range(HEADS // 2):
        e = END[("uq", j)]
        s += [(e, ("q_a", j)), (e + 1, ("q_b", j)), (e + 3, ("q_t", j))]
        e = END[("ukv", j)]
        s += [(e, ("k_a", j)), (e + 1, ("k_b", j)), (e + 3, ("k_t", j))]
    first = END[("ukv", 3)] + 5
    for h in range(HEADS):
        p = first + 3 * h
        s += [(p, ("scores", h)), (p + 1, ("softmax", h)), (p + 3, ("probs_t", h)), (p + 5, ("attend", h))]
    s += [(END[("hq", 1)] - 4, ("lb_a", 1)), (END[("hq", 1)] - 3, ("lb_b", 1))]
    for g in range(2):
        e = END[("hq", g)]
        s += [(e, ("hq", g))] + [(e + 2, ("turn", g, 0, t)) for t in range(NT)]
        e = END[("hf", g)]
        s += [(e, ("hf_a", g)), (e + 1, ("hf_b", g))]
        s += [(e + 3, ("turn", g, n, t)) for n in (1, 2) for t in range(NT)]
        p = e + 5
        s += [(p, ("pairs", g, 0))]
        for l in range(1, LEVELS + 1):
            s += [(p, ("lev_a", g, l)), (p + 1, ("lev_b", g, l)), (p + 3, ("pairs", g, l))]
            p += 3
        s += [(p + 1, ("join_a", g)), (p + 2, ("join_b", g)), (p + 4, ("join7", g)), (p + 5, ("join_c", g)),
              (p + 7, ("join8", g))]
        s += [(END[("hi", g)], ("hi", g)), (END[("hg", g)], ("hg", g))]
        p = max(p + 9, END[("hg", g)] + 2)
        s += [(p, ("o_a", g)), (p + 1, ("o_b", g)), (p + 4, ("o_t", g, 0)), (p + 4, ("o_t", g, 1))]
    for c in range(4):
        s += [(END[("out1", c)], ("out1", c))]
        e = END[("out2", c)]
        s += [(e, ("out2", c)), (e + 2, ("x2", c, 0)), (e + 2, ("x2", c, 1))]
    e = END[("out2", 3)]
    s += [(e + 3, ("r2a",)), (e + 4, ("r2b",))]
    return sorted(s, key=lambda x: x[0])


SCHEDULE = schedule()


def steps_at(position):
    return [step for p, step in SCHEDULE if p == position]


def side_uses(step):
    kind = step[0]
    if kind in ("x", "x2", "lat_t", "o_t"):
        return [(step, "dve")]
    if kind in ("vec", "turn", "probs_t", "join7", "join8"):
        return [(step, "act")]
    if kind in ("q_t", "k_t"):
        return [(step + (0,), "act"), (step + (1,), "act")]
    if kind in ("pairs", "o_a"):
        return [(step + (t,), "dve") for t in range(NT)]
    if kind in ("scores", "attend"):
        return [(step, "dve")]
    return []


USES = [u for _, step in SCHEDULE for u in side_uses(step)]
USE = {key: n for n, (key, _) in enumerate(USES)}
GIVEN, _given = {}, {"act": 0, "dve": 0}
for _, _step in SCHEDULE:
    if _step[0] != "o_a":
        for _key, _engine in side_uses(("o_a", _step[1]) if _step[0] == "o_b" else _step):
            _given[_engine] += 1
            GIVEN[USE[_key]] = _given[_engine]
SPLITS = [step for _, step in SCHEDULE if step[0] in ("x", "x2", "lat_t", "o_t", "attend")]
SPLIT = {step: n for n, step in enumerate(SPLITS)}


RMS = [step for _, step in SCHEDULE if step[0] in ("r1a", "lat_a", "q_a", "k_a", "o_a", "r2a")]


def squares_of(step):
    return {"r1a": 8, "lat_a": 2, "kr_a": 2, "q_a": 4, "k_a": 4, "o_a": NT * GH, "out2": NT}.get(step[0], 0)


SQUARES = {}
for _, _step in SCHEDULE:
    SQUARES[_step] = sum(squares_of(s) for s in SQUARES) + squares_of(_step)


def split_needed(g):
    b, k, n = GRANULES[g]
    kind, i = BLOCKS[b][:2]
    if kind == "cq":
        return SPLIT[("x", k // 2)] + 1
    if kind == "uq":
        return SPLIT[("lat_t", 0, 1)] + 1
    if kind == "ukv":
        return SPLIT[("lat_t", 1, 1)] + 1
    if kind == "out1":
        return max(SPLIT[("attend", HEADS - 1)], SPLIT[("o_t", 0, 1)]) + 1
    if kind == "out2":
        return SPLIT[("o_t", 1, 1)] + 1
    return SPLIT[("x", 7)] + 1


def hybrid_layer(nc, x, positions, attn_norm_w, w_in, hgrn_lb, hgrn_norm_w, mla_q_norm_w, w_uq, mla_kv_norm_w,
                 w_ukv, q_head_norm_w, k_head_norm_w, w_out, ffn_norm_w, w_gate_up, w_down, out):
    weights = {"w_in": w_in[0], "w_uq": w_uq[0], "w_ukv": w_ukv[0], "w_out": w_out[0]}
    w_gu = w_gate_up[0]
    w_dn = w_down[0]
    x_v = x[0].rearrange("(t p) d -> p t d", p=P)
    out_v = out[0].rearrange("(t p) d -> p t d", p=P)

    with ExitStack() as ctx:
        def sb(name, shape, dt=F32, where=ctx):
            return where.enter_context(nc.sbuf_tensor(name, shape, dt))

        def sem(name):
            return ctx.enter_context(nc.semaphore(name))

        raw = sb("raw", [P, RING, GRAN])
        w_hi = sb("w_hi", [P, RING, GRAN], F32R)
        w_lo = sb("w_lo", [P, RING, GRAN], F32R)
        hT_hi = sb("hT_hi", [P, KT, SEQ], F32R)
        hT_lo = sb("hT_lo", [P, KT, SEQ], F32R)
        X = sb("X", [P, NT, D])
        ident = sb("ident", [P, P])
        vec_cols = sb("vec_cols", [P, V_ROWS])
        junk = sb("junk", [P, QK])
        stat = sb("stat", [P, 64])
        r_in = stat[:, 0:2]
        r_ffn = stat[:, 2:4]
        sumsq = stat[:, 4:12]
        std = stat[:, 12:20]
        inv = stat[:, 20:28]
        sumsq_kr = stat[:, 28:30]
        top = stat[:, 30:34]
        shift = stat[:, 34:38]
        total_p = stat[:, 38:42]
        inv_p = stat[:, 42:46]
        sumsq_x = stat[:, 46:54]

        mix = ctx.enter_context(ExitStack())

        def mb(name, shape, dt=F32):
            return sb(name, shape, dt, mix)

        mT_hi = mb("mT_hi", [P, 12, SEQ], F32R)
        mT_lo = mb("mT_lo", [P, 12, SEQ], F32R)
        lat = mb("lat", [P, NT, LORA])
        stage = mb("stage", [P, 2, NT, 2, QK])
        stage_r = mb("stage_r", [P, 2, NT, 2, ROPE])
        rot = mb("rot", [P, 4, NT, 2, HALF])
        qTr = mb("qTr", [P, HEADS // 2, SEQ])
        kTr = mb("kTr", [P, HEADS // 2, SEQ])
        val = mb("val", [P, NT, HEADS, P])
        kr = mb("kr", [P, NT, ROPE])
        krw = mb("krw", [P, NT, ROPE])
        probs = mb("probs", [P, 2, 3 * P])
        probsT = mb("probsT", [P, 2, 3 * P])
        mask_add = mb("mask_add", [P, 2 * P])
        qw_row = mb("qw_row", [P, QK])
        kw_row = mb("kw_row", [P, QK])
        pos_i = mb("pos_i", [P, NT], I32)
        pos_f = mb("pos_f", [P, NT])
        freq = mb("freq", [P, HALF])
        sincos = mb("sincos", [P, 2, NT, HALF])
        turns = rot[:, 0, :, :, :]
        turns_hi = rot[:, 1, :, :, :]
        vec_rows = stage[0:V_ROWS, 0, 0, 0, 0:P]
        tri = mb("tri", [P, P])
        masks = mb("masks", [P, LEVELS, P])
        hq = lat
        hk = mb("hk", [P, NT, GW])
        hlf = mb("hlf", [P, NT, GW])
        hv = mb("hv", [P, NT, GW])
        hgate = mb("hgate", [P, NT, GW])
        hqT = mb("hqT", [P, GH, SEQ])
        hkT = mb("hkT", [P, GH, SEQ])
        hbT = mb("hbT", [P, GH, SEQ])
        E = mb("E", [P, 2, GH * SEQ])
        lb = E[:, 1, :].rearrange("p (n c) -> p n c", n=2)
        lb_tmp = hk[:, 0, :]
        wide_junk = hlf[:, 0, :]
        chunk_decay = mb("chunk_decay", [P, GH, SEQ // CHUNK])
        hS = mb("hS", [P, GH, 3, P])
        qTn = X[:, 0, :].rearrange("p (h t) -> p h t", h=HEADS)
        kTn = X[:, 1, :].rearrange("p (h t) -> p h t", h=HEADS)
        mix.close()

        aT_hi = sb("aT_hi", [P, DOWN_KT, SEQ], F32R)
        aT_lo = sb("aT_lo", [P, DOWN_KT, SEQ], F32R)
        gate = sb("gate", [P, NT, NB])
        hidden = sb("hidden", [P, NT, NB])

        main = [[ctx.enter_context(nc.psum_tensor(f"main{p}{t}", [P, NB], F32)) for t in range(NT)] for p in range(2)]
        side = [ctx.enter_context(nc.psum_tensor(f"side{n}", [P, NB], F32)) for n in range(SIDE)]

        s_raw = [sem(f"s_raw{i}") for i in range(RING)]
        s_hi = sem("s_hi")
        s_lo = sem("s_lo")
        s_used = sem("s_used")
        s_taken = [sem(f"s_taken{p}") for p in range(2)]
        s_side = sem("s_side")
        s_given = {"act": sem("s_given_act"), "dve": sem("s_given_dve")}
        s_thi = sem("s_thi")
        s_tlo = sem("s_tlo")
        s_x = [sem(f"s_x{c}") for c in range(4)]
        s_small = sem("s_small")
        s_lbin = sem("s_lbin")
        s_lbused = sem("s_lbused")
        s_xagain = sem("s_xagain")
        s_const = sem("s_const")
        s_dchain = sem("s_dchain")
        s_sq = sem("s_sq")
        s_mean = sem("s_mean")
        s_std = sem("s_std")
        s_inv = sem("s_inv")
        s_angle = sem("s_angle")
        s_sin = sem("s_sin")
        s_lbmax = sem("s_lbmax")
        s_lbexp = sem("s_lbexp")
        s_stage = sem("s_stage")
        s_val = sem("s_val")
        s_top = sem("s_top")
        s_exp = sem("s_exp")
        s_prob = sem("s_prob")
        s_f = sem("s_f")
        s_logf = sem("s_logf")
        s_arg = sem("s_arg")
        s_dec = sem("s_dec")
        s_lev = sem("s_lev")
        s_join = sem("s_join")
        s_turned = sem("s_turned")
        s_ahi = sem("s_ahi")
        s_alo = sem("s_alo")
        s_out = sem("s_out")

        block = ctx.enter_context(nc.Block())

        FF = len(BLOCKS)
        DOWN = FF + 2 * NFF
        PG, PU = FF % 2, (FF + 1) % 2

        def taken(b):
            return NT * (b // 2 + 1)

        def bank(n):
            return side[n % SIDE]

        N_SMALL = 8
        N_IDENT = 2
        N_CONST = 2 + 3 + 1 + 3 * LEVELS + 1 + 2 + HALF

        @block.sync
        def _(sp):
            def slot_free(g):
                sp.wait_ge(s_hi, g - RING + 1)
                sp.wait_ge(s_lo, g - RING + 1)

            def load_x(c):
                sp.dma_start(X[:, :, c * NB:(c + 1) * NB], x_v[:, :, c * NB:(c + 1) * NB]).then_inc(s_x[c], 16)

            load_x(0)
            for g, (b, k, n) in enumerate(GRANULES):
                kind, i, w, c0, cols, rows, _ = BLOCKS[b]
                if g >= RING:
                    slot_free(g)
                src = weights[w][rows[k]:rows[k] + n * P, c0:c0 + cols].rearrange("(k p) c -> p k c", p=P)
                dst = raw[:, g % RING, 0:n * cols].rearrange("p (k c) -> p k c", k=n)
                sp.dma_start(dst, src).then_inc(s_raw[g % RING], 16)
                if g < 3:
                    load_x(g + 1)
            with sp.Fori(0, NFF) as i:
                for half in range(2):
                    for k in range(KT // 2):
                        j = half * (KT // 2) + k
                        slot = (G0 + j) % RING
                        slot_free(G0 + j + GU * i)
                        src = w_gu[2 * P * k:2 * P * (k + 1), bass.ds(half * D_FF + NB * i, NB)]
                        sp.dma_start(raw[:, slot, :].rearrange("p (k c) -> p k c", k=2),
                                     src.rearrange("(k p) c -> p k c", p=P)).then_inc(s_raw[slot], 16)
            with sp.Fori(0, 2) as i:
                for j in range(2 * DN):
                    slot = (G1 + j) % RING
                    slot_free(G1 + j + 2 * DN * i)
                    k = j % DN
                    src = w_dn[2 * P * k:2 * P * (k + 1), bass.ds(NB * (j // DN) + 2 * NB * i, NB)]
                    sp.dma_start(raw[:, slot, :].rearrange("p (k c) -> p k c", k=2),
                                 src.rearrange("(k p) c -> p k c", p=P)).then_inc(s_raw[slot], 16)
            for d in range(4):
                sp.wait_ge(s_taken[(DOWN + d) % 2], taken(DOWN + d))
                cols = slice(d * NB, (d + 1) * NB)
                sp.dma_start(out_v[:, :, cols], X[:, :, cols]).then_inc(s_out, 16)
            sp.wait_ge(s_out, 4 * 16)

        @block.gpsimd
        def _(pool):
            made = [0]

            def done(ins):
                made[0] += 1
                ins.then_inc(s_const, 1)

            def settle():
                pool.wait_ge(s_const, made[0])

            done(pool.memset(ident[:, :], 0.0))
            settle()
            done(pool.affine_select(out=ident[:, :], in_=ident[:, :], compare_op=ALU.not_equal, fill=1.0, base=0,
                                    pattern=[[-1, P]], channel_multiplier=1))
            pool.dma_start(lb[:, :, :], hgrn_lb[:, 0:GW].partition_broadcast(P)).then_inc(s_lbin, 16)
            done(pool.memset(mask_add[:, :], 0.0))
            settle()
            done(pool.memset(mask_add[0:CHUNK, 2 * P - CHUNK:2 * P], MASKED))
            for n in range(HALF):
                f = np.float32(1.0) / np.power(np.float32(10000.0), np.float32(2 * n) / np.float32(ROPE))
                done(pool.memset(freq[:, n:n + 1], float(f)))
            v = tri[:, :].rearrange("p (c t) -> p c t", c=2)
            done(pool.memset(tri[:, :], 1.0))
            settle()
            done(pool.affine_select(out=v, in_=v, compare_op=ALU.is_ge, fill=0.0, base=0,
                                    pattern=[[CHUNK, 2], [1, CHUNK]], channel_multiplier=-1))
            settle()
            done(pool.affine_select(out=v, in_=v, compare_op=ALU.is_ge, fill=0.0, base=0,
                                    pattern=[[-CHUNK, 2], [0, CHUNK]], channel_multiplier=1))
            done(pool.memset(masks[:, :, :], 0.0))
            settle()
            for l in range(1, LEVELS + 1):
                h = 1 << (l - 1)
                n = P // (2 * h)
                v = masks[:, l - 1, :].rearrange("p (n two h) -> p n two h", two=2, h=h)[:, :, 1, :]
                done(pool.memset(v, 1.0))
                settle()
                done(pool.affine_select(out=v, in_=v, compare_op=ALU.is_ge, fill=0.0, base=0,
                                        pattern=[[-2 * h, n], [0, h]], channel_multiplier=1))
                settle()
                done(pool.affine_select(out=v, in_=v, compare_op=ALU.is_ge, fill=0.0, base=h - 1,
                                        pattern=[[2 * h, n], [0, h]], channel_multiplier=-1))
            done(pool.memset(hS[:, :, :, :], 0.0))
            pool.wait_ge(s_lbused, 1)
            pool.wait_ge(s_side, USE[("join8", 0)] + 1)
            pool.dma_start(lb[:, :, :], hgrn_lb[:, GW:2 * GW].partition_broadcast(P)).then_inc(s_lbin, 16)
            pool.wait_ge(s_side, USE[("scores", HEADS - 1)] + 1)
            pool.dma_start(X[:, :, :], x_v).then_inc(s_xagain, 16)

        @block.scalar
        def _(act):
            activation = nc.scalar.activation
            copy = nc.scalar.copy

            def convert(slot, loads, g, n=GRAN):
                act.wait_ge(s_raw[slot], 16 * loads)
                if not isinstance(g, int) or g >= RING:
                    act.wait_ge(s_used, g - RING + 1)
                copy(w_hi[:, slot, 0:n], raw[:, slot, 0:n]).then_inc(s_hi, 1)

            def block_banks(kind, i):
                act.wait_ge(s_used, END[(kind, i)])
                b = BLOCK_OF[(kind, i)]
                return main[b % 2], s_taken[b % 2]

            def filled(key):
                act.wait_ge(s_side, USE[key] + 1)
                return bank(USE[key])

            n_squares = [0]

            def square(src, total, **kw):
                if n_squares[0]:
                    act.wait_ge(s_sq, n_squares[0])
                n_squares[0] += 1
                n = src.shape[-1]
                activation((junk if n <= QK else wide_junk)[:, 0:n], src, ACT.Square, accum_out=total, **kw).then_inc(s_sq, 1)

            def sums_free(step):
                if RMS.index(step):
                    act.wait_ge(s_mean, RMS.index(step))

            def root(step, n):
                act.wait_ge(s_mean, RMS.index(step) + 1)
                activation(std[:, 0:n], std[:, 0:n], ACT.Sqrt).then_inc(s_std, 1)

            def split_hi(parts):
                for dst, src, col in parts:
                    if col is None:
                        ins = copy(dst, src)
                    else:
                        ins = activation(dst, src, ACT.Copy, scale=vec_cols[:, col:col + 1])
                ins.then_inc(s_thi, 1)

            def small_loads():
                rows = ((V_ATTN, attn_norm_w), (V_FFN, ffn_norm_w), (V_QN, mla_q_norm_w), (V_KVN, mla_kv_norm_w),
                        (V_HG, hgrn_norm_w))
                for r, w in rows:
                    v = w.rearrange("a (k p) -> (a k) p", p=P)
                    act.dma_start(vec_rows[r:r + v.shape[0], :], v).then_inc(s_small, 16)
                act.dma_start(pos_i[:, :], positions[0].rearrange("(t p) -> p t", p=P),
                              allow_slow_non_contiguous=True).then_inc(s_small, 16)
                act.dma_start(qw_row[:, :], q_head_norm_w[0].partition_broadcast(P)).then_inc(s_small, 16)
                act.dma_start(kw_row[:, :], k_head_norm_w[0].partition_broadcast(P)).then_inc(s_small, 16)

            def step(s):
                kind, a = s[0], s[1:]
                if kind == "vec":
                    copy(vec_cols[:, :], filled(s)[:, 0:V_ROWS]).then_inc(s_given["act"], 1)
                    act.wait_ge(s_given["act"], 1)
                elif kind == "x":
                    ps, k = filled(s), 2 * a[0]
                    split_hi([(hT_hi[:, k + n, :], ps[:, n * SEQ:(n + 1) * SEQ], V_ATTN + k + n) for n in range(2)])
                elif kind == "r1a":
                    for c in range(4):
                        act.wait_ge(s_x[c], 16)
                    for t in range(NT):
                        for c in range(4):
                            square(X[:, t, c * NB:(c + 1) * NB], sumsq[:, 4 * t + c:4 * t + c + 1])
                elif kind == "r1b":
                    root(("r1a",), NT)
                elif kind == "sines":
                    act.wait_ge(s_angle, 1)
                    activation(sincos[:, :, :, :], sincos[:, :, :, :], ACT.Sin).then_inc(s_sin, 1)
                elif kind == "lat_a":
                    ps, _ = block_banks("ckv" if a[0] else "cq", 0)
                    sums_free(s)
                    act.wait_ge(s_inv, 1)
                    for t in range(NT):
                        square(ps[t][:, :], sumsq[:, t:t + 1], scale=r_in[:, t:t + 1])
                elif kind == "lat_b":
                    root(("lat_a",) + a, NT)
                elif kind == "lat_t":
                    i, j = a
                    ps, k, col = filled(s), 4 * i + 2 * j, (V_KVN if i else V_QN) + 2 * j
                    split_hi([(mT_hi[:, k + n, :], ps[:, n * SEQ:(n + 1) * SEQ], col + n) for n in range(2)])
                elif kind == "kr_a":
                    ps, _ = block_banks("kr", 0)
                    for t in range(NT):
                        square(ps[t][:, 0:ROPE], sumsq_kr[:, t:t + 1], scale=r_in[:, t:t + 1])
                elif kind == "lb_b":
                    act.wait_ge(s_lbmax, a[0] + 1)
                    activation(lb[:, :, :], lb[:, :, :], ACT.Exp).then_inc(s_lbexp, 1)
                elif kind in ("q_a", "k_a"):
                    ps, _ = block_banks("uq" if kind == "q_a" else "ukv", a[0])
                    width, stride = (QK, QK) if kind == "q_a" else (NOPE, NOPE + P)
                    sums_free(s)
                    for t in range(NT):
                        for h in range(2):
                            square(ps[t][:, h * stride:h * stride + width], sumsq[:, 2 * t + h:2 * t + h + 1])
                elif kind in ("q_b", "k_b"):
                    root((kind[0] + "_a",) + a, 2 * NT)
                    if kind == "k_b":
                        ps, _ = block_banks("ukv", a[0])
                        for t in range(NT):
                            src = ps[t][:, :].rearrange("p (h c) -> p h c", h=2)[:, :, NOPE:NOPE + P]
                            copy(val[:, t, 2 * a[0]:2 * a[0] + 2, :], src).then_inc(s_val, 1)
                elif kind in ("q_t", "k_t"):
                    j = a[0]
                    plain, rotated = (qTn, qTr) if kind == "q_t" else (kTn, kTr)
                    copy(plain[:, 2 * j:2 * j + 2, :], filled(s + (0,))[:, :].rearrange("p (h t) -> p h t", h=2))\
                        .then_inc(s_given["act"], 1)
                    copy(rotated[:, j, :], filled(s + (1,))[:, 0:SEQ]).then_inc(s_given["act"], 1)
                elif kind == "softmax":
                    h, b = a[0], a[0] % 2
                    act.wait_ge(s_top, h + 1)
                    for t, (lo, hi) in enumerate(((0, P), (P, 3 * P))):
                        activation(probs[:, b, lo:hi], probs[:, b, lo:hi], ACT.Exp, scale=SCALE,
                                   bias=shift[:, 2 * b + t:2 * b + t + 1],
                                   accum_out=total_p[:, 2 * b + t:2 * b + t + 1]).then_inc(s_exp, 1)
                elif kind == "probs_t":
                    copy(probsT[:, a[0] % 2, :], filled(s)[:, 0:3 * P]).then_inc(s_given["act"], 1)
                elif kind == "attend":
                    split_hi([(mT_hi[:, 4 + a[0], :], filled(s)[:, 0:SEQ], None)])
                elif kind in ("hq", "hf_a", "hi", "hg"):
                    ps, read = block_banks(kind[:2], a[0])
                    dst, fn = {"hq": (hq, ACT.Silu), "hf_a": (hlf, ACT.Sigmoid), "hi": (hv, ACT.Copy),
                               "hg": (hgate, ACT.Silu)}[kind]
                    if kind == "hq" and not a[0]:
                        act.wait_ge(s_side, USE[("lat_t", 1, 1)] + 1)
                    if a[0] and kind == "hg":
                        act.wait_ge(s_given["dve"], GIVEN[USE[("o_a", 0, NT - 1)]])
                    for t in range(NT):
                        activation(dst[:, t, :], ps[t][:, :], fn, scale=r_in[:, t:t + 1]).then_inc(read, 1)
                elif kind == "hf_b":
                    act.wait_ge(s_f, a[0] + 1)
                    activation(hlf[:, :, :], hlf[:, :, :], ACT.Ln).then_inc(s_logf, 1)
                elif kind == "turn":
                    g, n, t = a
                    if g:
                        act.wait_ge(s_join, g)
                    copy((hqT, hkT, hbT)[n][:, :, t * P:(t + 1) * P],
                         filled(s)[:, :].rearrange("p (h t) -> p h t", h=GH)).then_inc(s_given["act"], 1)
                elif kind == "lev_b":
                    g, l = a
                    act.wait_ge(s_arg, (LEVELS + 1) * g + l)
                    v = E[:, l % 2, :].rearrange("p (n two h) -> p n two h", two=2, h=1 << (l - 1))
                    activation(v[:, :, 0, :], v[:, :, 0, :], ACT.Exp, scale=-1.0)
                    activation(v[:, :, 1, :], v[:, :, 1, :], ACT.Exp).then_inc(s_dec, 1)
                elif kind == "join_b":
                    act.wait_ge(s_arg, (LEVELS + 1) * (a[0] + 1))
                    activation(E[:, 0, :], E[:, 0, :], ACT.Exp, scale=-1.0)
                    activation(E[:, 1, :], hbT[:, :, :].rearrange("p h t -> p (h t)"), ACT.Exp)
                    ends = hbT[:, :, :].rearrange("p h (c t) -> p h c t", t=CHUNK)[:, :, :, CHUNK - 1]
                    activation(chunk_decay[:, :, :], ends, ACT.Exp).then_inc(s_dec, 1)
                elif kind == "join7":
                    src = filled(s)[0:CHUNK, :].rearrange("p (h t c) -> p h t c", h=GH, t=2)
                    copy(hS[0:CHUNK, :, 0:2, CHUNK:P], src).then_inc(s_given["act"], 1)
                elif kind == "join8":
                    copy(hS[:, :, 2, :], filled(s)[:, :].rearrange("p (h t) -> p h t", h=GH))\
                        .then_inc(s_given["act"], 1)
                elif kind == "o_a":
                    sums_free(s)
                    for t in range(NT):
                        ps = filled(s + (t,))
                        for h in range(GH):
                            square(ps[:, h * P:(h + 1) * P], sumsq[:, GH * t + h:GH * t + h + 1])
                elif kind == "o_b":
                    root(("o_a",) + a, NT * GH)
                elif kind == "o_t":
                    g, j = a
                    dst, k = (hT_hi, 12 + 2 * j) if g else (mT_hi, 2 * j)
                    split_hi([(dst[:, k:k + 2, :], filled(s)[:, :].rearrange("p (k t) -> p k t", k=2), V_HG)])
                elif kind == "out2":
                    c = a[0]
                    b = BLOCK_OF[s]
                    act.wait_ge(s_taken[b % 2], taken(b))
                    for t in range(NT):
                        square(X[:, t, c * NB:(c + 1) * NB], sumsq_x[:, 4 * t + c:4 * t + c + 1])
                elif kind == "x2":
                    ps, k = filled(s), 4 * a[0] + 2 * a[1]
                    split_hi([(hT_hi[:, k + n, :], ps[:, n * SEQ:(n + 1) * SEQ], V_FFN + k + n) for n in range(2)])
                elif kind == "r2b":
                    root(("r2a",), NT)

            def silu(i):
                act.wait_ge(s_used, G0 + KT // 2 + GU * i)
                for t in range(NT):
                    activation(gate[:, t, :], main[PG][t][:, :], ACT.Silu, scale=r_ffn[:, t:t + 1])\
                        .then_inc(s_taken[PG], 1)

            def split_hidden(i):
                for u in range(2):
                    act.wait_ge(s_turned, 2 * i + u + 1)
                    copy(aT_hi[:, bass.ds(4 * i + 2 * u, 2), :],
                         side[u][:, :].rearrange("p (k t) -> p k t", k=2)).then_inc(s_ahi, 1)

            small_loads()
            for s in steps_at(-1):
                step(s)
            for g in range(LEAD):
                convert(g % RING, g // RING + 1, g, granule_size(g))
            for g in range(G0):
                n = g + LEAD
                convert(n % RING, n // RING + 1, n, granule_size(n))
                for s in steps_at(g):
                    step(s)
            for j in range(GU):
                n = G0 + j + LEAD
                convert(n % RING, n // RING + 1, n)
                for s in steps_at(G0 + j):
                    step(s)
                if j == KT // 2:
                    act.wait_ge(s_inv, len(RMS))
                    silu(0)
            with act.Fori(1, NFF) as i:
                for j in range(GU):
                    n = G0 + j + LEAD
                    convert(n % RING, n // RING + 1 + (GU // RING) * i, n + GU * i)
                    if j == 3:
                        split_hidden(i - 1)
                    if j == KT // 2:
                        act.wait_ge(s_taken[PU], taken(FF + 1) + NT * (i - 1))
                        silu(i)
            split_hidden(NFF - 1)
            for n in range(G1 + LEAD, G1 + 4 * DN):
                convert(n % RING, n // RING + 1, n)

        @block.vector
        def _(dve):
            tt, ts, stt = nc.vector.tensor_tensor, nc.vector.tensor_scalar, nc.vector.scalar_tensor_tensor
            chain = [0]

            def link(ins):
                chain[0] += 1
                ins.then_inc(s_dchain, 1)
                dve.wait_ge(s_dchain, chain[0])

            def convert(slot, g, n=GRAN):
                dve.wait_ge(s_hi, g + 1)
                tt(w_lo[:, slot, 0:n], raw[:, slot, 0:n], w_hi[:, slot, 0:n].bitcast(F32), ALU.subtract)\
                    .then_inc(s_lo, 1)

            def block_banks(kind, i):
                dve.wait_ge(s_used, END[(kind, i)])
                b = BLOCK_OF[(kind, i)]
                return main[b % 2], s_taken[b % 2]

            def filled(key):
                dve.wait_ge(s_side, USE[key] + 1)
                return bank(USE[key])

            def split_lo(s, parts):
                dve.wait_ge(s_thi, SPLIT[s] + 1)
                for dst, src, hi, col in parts:
                    if col is None:
                        ins = tt(dst, src, hi.bitcast(F32), ALU.subtract)
                    else:
                        ins = stt(out=dst, in0=src, scalar=vec_cols[:, col:col + 1], in1=hi.bitcast(F32),
                                  op0=ALU.mult, op1=ALU.subtract)
                ins.then_inc(s_tlo, 1)
                dve.wait_ge(s_tlo, SPLIT[s] + 1)
                dve.sem_inc(s_given["dve"], 1)

            def mean(n, width):
                ts(std[:, 0:n], std[:, 0:n], 1.0 / width, EPS, ALU.mult, ALU.add).then_inc(s_mean, 1)

            def sums(s):
                dve.wait_ge(s_sq, SQUARES[s])

            def reciprocal(s, dst, n):
                dve.wait_ge(s_std, RMS.index(s) + 1)
                nc.vector.reciprocal(dst, std[:, 0:n]).then_inc(s_inv, 1)
                dve.wait_ge(s_inv, RMS.index(s) + 1)

            def rotate(dst, src):
                n = src.shape[2]
                a, b = src[:, :, :, 0:HALF], src[:, :, :, HALF:ROPE]
                sin = sincos[:, 0, :, :].unsqueeze(2).to_broadcast([P, NT, n, HALF])
                cos = sincos[:, 1, :, :].unsqueeze(2).to_broadcast([P, NT, n, HALF])
                r = [rot[:, m, :, 0:n, :] for m in range(4)]
                tt(r[0], a, cos, ALU.mult)
                tt(r[1], b, sin, ALU.mult)
                tt(r[2], a, sin, ALU.mult)
                link(tt(r[3], b, cos, ALU.mult))
                tt(dst[:, :, :, 0:HALF], r[0], r[1], ALU.subtract)
                return tt(dst[:, :, :, HALF:ROPE], r[2], r[3], ALU.add)

            def angles():
                dve.wait_ge(s_small, 16 * N_SMALL)
                dve.wait_ge(s_const, N_CONST)
                link(nc.vector.tensor_copy(pos_f[:, :], pos_i[:, :]))
                for t in range(NT):
                    for f in range(2):
                        ins = ts(sincos[:, f, t, :], freq[:, :], pos_f[:, t:t + 1], None, ALU.mult)
                link(ins)
                to_int = 1.5 * 2.0 ** 23
                far = 4096.0
                for f, quarter in ((0, 0.0), (1, 0.25)):
                    ins = ts(turns[:, f, :, :], sincos[:, f, :, :], 1.0 / (2.0 * np.pi), quarter, ALU.mult, ALU.add)
                link(ins)
                link(ts(turns[:, :, :, :], turns[:, :, :, :], to_int, to_int, ALU.add, ALU.subtract))
                link(ts(turns_hi[:, :, :, :], turns[:, :, :, :], 1.0 / far, to_int, ALU.mult, ALU.add))
                link(ts(turns_hi[:, :, :, :], turns_hi[:, :, :, :], to_int, far, ALU.subtract, ALU.mult))
                link(tt(turns[:, :, :, :], turns[:, :, :, :], turns_hi[:, :, :, :], ALU.subtract))
                two_pi = 2.0 * np.pi
                c1 = np.floor(two_pi * 2 ** 9) / 2 ** 9
                c2 = np.floor((two_pi - c1) * 2 ** 21) / 2 ** 21
                c3 = two_pi - c1 - c2
                for c in (c1, c2, c3):
                    for n in (turns_hi, turns):
                        flat = [v[:, :, :, :].rearrange("p f t h -> p (f t h)") for v in (sincos, n)]
                        link(stt(out=flat[0], in0=flat[1], scalar=-float(c), in1=flat[0], op0=ALU.mult, op1=ALU.add))
                link(ts(sincos[:, 1, :, :], sincos[:, 1, :, :], float(np.pi / 2), None, ALU.add))
                pi = 3.1415925
                ts(sincos[:, :, :, :], sincos[:, :, :, :], pi, -pi, ALU.min, ALU.max).then_inc(s_angle, 1)

            def step(s):
                kind, a = s[0], s[1:]
                if kind == "x":
                    ps, k = filled(s), 2 * a[0]
                    split_lo(s, [(hT_lo[:, k + n, :], ps[:, n * SEQ:(n + 1) * SEQ], hT_hi[:, k + n, :],
                                  V_ATTN + k + n) for n in range(2)])
                elif kind in ("r1a", "r2a"):
                    src = sumsq if kind == "r1a" else sumsq_x
                    sums(s)
                    link(nc.vector.tensor_reduce(std[:, 0:NT], src[:, :].rearrange("p (t c) -> p t c", t=NT), AX.X,
                                                 ALU.add))
                    mean(NT, D)
                elif kind == "r1b":
                    reciprocal(("r1a",), r_in[:, :], NT)
                elif kind == "r2b":
                    reciprocal(("r2a",), r_ffn[:, :], NT)
                elif kind == "angles":
                    angles()
                elif kind == "lat_a":
                    sums(s)
                    ts(std[:, 0:NT], sumsq[:, 0:NT], 1.0 / LORA, EPS, ALU.mult, ALU.add).then_inc(s_mean, 1)
                elif kind == "lat_b":
                    ps, read = block_banks("ckv" if a[0] else "cq", 0)
                    reciprocal(("lat_a",) + a, inv[:, 0:NT], NT)
                    link(tt(inv[:, 0:NT], inv[:, 0:NT], r_in[:, :], ALU.mult))
                    if a[0]:
                        dve.wait_ge(s_side, USE[("lat_t", 0, 1)] + 1)
                    for t in range(NT):
                        ts(lat[:, t, :], ps[t][:, :], inv[:, t:t + 1], None, ALU.mult).then_inc(read, 1)
                elif kind == "lat_t":
                    i, j = a
                    ps, k, col = filled(s), 4 * i + 2 * j, (V_KVN if i else V_QN) + 2 * j
                    split_lo(s, [(mT_lo[:, k + n, :], ps[:, n * SEQ:(n + 1) * SEQ], mT_hi[:, k + n, :], col + n)
                                 for n in range(2)])
                elif kind == "kr_b":
                    ps, read = block_banks("kr", 0)
                    sums(("kr_a",))
                    for t in range(NT):
                        stt(out=krw[:, t, :], in0=ps[t][:, 0:ROPE], scalar=r_in[:, t:t + 1], in1=kw_row[:, NOPE:QK],
                            op0=ALU.mult, op1=ALU.mult).then_inc(read, 1)
                    dve.wait_ge(read, taken(BLOCK_OF[("kr", 0)]))
                    dve.wait_ge(s_sin, 1)
                    link(rotate(kr[:, :, :].unsqueeze(2), krw[:, :, :].unsqueeze(2)))
                elif kind == "lb_a":
                    dve.wait_ge(s_lbin, 16 * (a[0] + 1))
                    link(tt(lb_tmp[:, :], lb[:, 0, :], lb[:, 1, :], ALU.max))
                    tt(lb[:, 0, :], lb[:, 0, :], lb_tmp[:, :], ALU.subtract)
                    tt(lb[:, 1, :], lb[:, 1, :], lb_tmp[:, :], ALU.subtract).then_inc(s_lbmax, 1)
                elif kind == "lb_b":
                    dve.wait_ge(s_lbexp, a[0] + 1)
                    link(tt(lb_tmp[:, :], lb[:, 0, :], lb[:, 1, :], ALU.add))
                    link(nc.vector.reciprocal(lb_tmp[:, :], lb_tmp[:, :]))
                    link(tt(lb[:, 0, :], lb[:, 0, :], lb_tmp[:, :], ALU.mult))
                    link(ts(lb[:, 1, :], lb[:, 0, :], -1.0, 1.0, ALU.mult, ALU.add))
                    link(ts(lb[:, 0, :], lb[:, 0, :], 1e-19, None, ALU.max))
                elif kind == "q_a":
                    sums(s)
                    ts(std[:, 0:4], sumsq[:, 0:4], 1.0 / QK, EPS, ALU.mult, ALU.add).then_inc(s_mean, 1)
                elif kind == "k_a":
                    sums(s)
                    link(tt(std[:, 0:4].rearrange("p (t h) -> p t h", t=NT),
                            sumsq[:, 0:4].rearrange("p (t h) -> p t h", t=NT),
                            sumsq_kr[:, :].unsqueeze(2).to_broadcast([P, NT, 2]), ALU.add))
                    mean(4, QK)
                elif kind in ("q_b", "k_b"):
                    j, b = a[0], a[0] % 2
                    ps, read = block_banks("uq" if kind == "q_b" else "ukv", j)
                    reciprocal((kind[0] + "_a",) + a, inv[:, 0:4], 4)
                    before = ("q_t", j - 2) if kind == "q_b" else (("k_t", j - 2) if j > 1 else ("q_t", j + 2))
                    if before[1] >= 0:
                        dve.wait_ge(s_side, USE[before + (1,)] + 1)
                    if kind == "q_b":
                        for t in range(NT):
                            for h in range(2):
                                ins = stt(out=stage[:, b, t, h, :], in0=ps[t][:, h * QK:(h + 1) * QK],
                                          scalar=inv[:, 2 * t + h:2 * t + h + 1], in1=qw_row[:, :],
                                          op0=ALU.mult, op1=ALU.mult)
                            ins.then_inc(read, 1)
                        dve.wait_ge(read, taken(BLOCK_OF[("uq", j)]))
                        rotate(stage_r[:, b, :, :, :], stage[:, b, :, :, NOPE:QK]).then_inc(s_stage, 1)
                    else:
                        dve.wait_ge(s_val, NT * (j + 1))
                        for t in range(NT):
                            for h in range(2):
                                at = h * (NOPE + P)
                                ins = stt(out=stage[:, b, t, h, 0:NOPE], in0=ps[t][:, at:at + NOPE],
                                          scalar=inv[:, 2 * t + h:2 * t + h + 1], in1=kw_row[:, 0:NOPE],
                                          op0=ALU.mult, op1=ALU.mult)
                            ins.then_inc(read, 1)
                        for t in range(NT):
                            for h in range(2):
                                ins = ts(stage_r[:, b, t, h, :], kr[:, t, :], inv[:, 2 * t + h:2 * t + h + 1], None,
                                         ALU.mult)
                        ins.then_inc(s_stage, 1)
                elif kind == "scores":
                    h, b = a[0], a[0] % 2
                    ps = filled(s)
                    if h >= 2:
                        dve.wait_ge(s_side, USE[("probs_t", h - 2)] + 1)
                    for t, (lo, hi) in enumerate(((0, P), (P, 3 * P))):
                        ins = nc.vector.tensor_tensor_reduce(
                            out=probs[:, b, lo:hi], in0=ps[:, lo:hi], in1=mask_add[:, 2 * P - (hi - lo):2 * P], scale=1.0,
                            scalar=-3.0e38, op0=ALU.add, op1=ALU.max, accum_out=top[:, 2 * b + t:2 * b + t + 1])
                    ins.then_inc(s_given["dve"], 1)
                    dve.wait_ge(s_given["dve"], GIVEN[USE[s]])
                    ts(shift[:, 2 * b:2 * b + 2], top[:, 2 * b:2 * b + 2], -SCALE, None, ALU.mult).then_inc(s_top, 1)
                elif kind == "softmax":
                    h, b = a[0], a[0] % 2
                    dve.wait_ge(s_exp, NT * (h + 1))
                    link(nc.vector.reciprocal(inv_p[:, 2 * b:2 * b + 2], total_p[:, 2 * b:2 * b + 2]))
                    for t, (lo, hi) in enumerate(((0, P), (P, 3 * P))):
                        ins = ts(probs[:, b, lo:hi], probs[:, b, lo:hi], inv_p[:, 2 * b + t:2 * b + t + 1], None,
                                 ALU.mult)
                    ins.then_inc(s_prob, 1)
                elif kind == "attend":
                    k = 4 + a[0]
                    split_lo(s, [(mT_lo[:, k, :], filled(s)[:, 0:SEQ], mT_hi[:, k, :], None)])
                elif kind == "hf_a":
                    g = a[0]
                    b = BLOCK_OF[("hf", g)]
                    dve.wait_ge(s_taken[b % 2], taken(b))
                    if g:
                        dve.wait_ge(s_side, USE[("turn", 0, 1, NT - 1)] + 1)
                    wide = [lb[:, n, :].unsqueeze(1).to_broadcast([P, NT, GW]) for n in range(2)]
                    link(tt(hlf[:, :, :], hlf[:, :, :], wide[1], ALU.mult))
                    tt(hlf[:, :, :], hlf[:, :, :], wide[0], ALU.add).then_inc(s_lbused, 1)
                    dve.wait_ge(s_lbused, g + 1)
                    ts(hk[:, :, :], hlf[:, :, :], -1.0, 1.0, ALU.mult, ALU.add).then_inc(s_f, 1)
                elif kind == "lev_a":
                    g, l = a
                    dve.wait_ge(s_given["act"], GIVEN[USE[("turn", g, 2, NT - 1)]])
                    if l > 2:
                        dve.wait_ge(s_side, USE[("pairs", g, l - 2, NT - 1)] + 1)
                    elif g:
                        dve.wait_ge(s_side, USE[("o_t", g - 1, 1)] + 1)
                    h = 1 << (l - 1)
                    n = GH * SEQ // (2 * h)
                    b_ = hbT[:, :, :].rearrange("p a t -> p (a t)").rearrange("p (n w) -> p n w", w=2 * h)
                    mid = b_[:, :, h - 1:h].to_broadcast([P, n, 2 * h])
                    tt(E[:, l % 2, :].rearrange("p (n w) -> p n w", w=2 * h), b_, mid, ALU.subtract)\
                        .then_inc(s_arg, 1)
                elif kind == "lev_b":
                    g, l = a
                    dve.wait_ge(s_dec, (LEVELS + 1) * g + l)
                    e, k_, q_ = [v.rearrange("p (n two h) -> p n two h", two=2, h=1 << (l - 1)) for v in
                                 (E[:, l % 2, :], hkT[:, :, :].rearrange("p a t -> p (a t)"),
                                  hqT[:, :, :].rearrange("p a t -> p (a t)"))]
                    tt(e[:, :, 0, :], e[:, :, 0, :], k_[:, :, 0, :], ALU.mult)
                    tt(e[:, :, 1, :], e[:, :, 1, :], q_[:, :, 1, :], ALU.mult).then_inc(s_lev, 1)
                elif kind == "pairs":
                    g, l = a
                    mask = (ident[:, :] if l == 0 else masks[:, l - 1, :]).bitcast(I32)
                    for t in range(NT):
                        ps = filled(s + (t,))
                        n = USE[s + (t,)]
                        if GIVEN[n] > 1:
                            dve.wait_ge(s_given["dve"], GIVEN[n] - 1)
                        nc.vector.copy_predicated(hS[:, :, t, :], mask.unsqueeze(1).to_broadcast([P, GH, P]),
                                                  ps[:, :].rearrange("p (h t) -> p h t", h=GH))\
                            .then_inc(s_given["dve"], 1)
                elif kind == "join_a":
                    g = a[0]
                    dve.wait_ge(s_side, USE[("pairs", g, LEVELS, NT - 1)] + 1)
                    b_ = hbT[:, :, :].rearrange("p h (c t) -> p (h c) t", t=CHUNK)
                    last = b_[:, :, CHUNK - 1:CHUNK].to_broadcast([P, GH * SEQ // CHUNK, CHUNK])
                    tt(E[:, 0, :].rearrange("p (n t) -> p n t", t=CHUNK), b_, last, ALU.subtract).then_inc(s_arg, 1)
                elif kind == "join_b":
                    g = a[0]
                    dve.wait_ge(s_dec, (LEVELS + 1) * (g + 1))
                    tt(E[:, 0, :], E[:, 0, :], hkT[:, :, :].rearrange("p a t -> p (a t)"), ALU.mult)
                    tt(E[:, 1, :], E[:, 1, :], hqT[:, :, :].rearrange("p a t -> p (a t)"), ALU.mult)\
                        .then_inc(s_lev, 1)
                    dve.wait_ge(s_lev, (LEVELS + 1) * (g + 1))
                elif kind == "join_c":
                    g = a[0]
                    dve.wait_ge(s_side, USE[("join7", g)] + 1)
                    v = E[:, 0, :].rearrange("p (h t) -> p h t", h=GH)[:, :, 0:CHUNK]
                    tt(v, v, chunk_decay[:, :, 1:2].to_broadcast([P, GH, CHUNK]), ALU.mult)
                    v = E[:, 1, :].rearrange("p (h t) -> p h t", h=GH)[:, :, 3 * CHUNK:SEQ]
                    tt(v, v, chunk_decay[:, :, 2:3].to_broadcast([P, GH, CHUNK]), ALU.mult).then_inc(s_join, 1)
                elif kind == "o_a":
                    sums(s)
                    ts(std[:, 0:NT * GH], sumsq[:, 0:NT * GH], 1.0 / P, EPS, ALU.mult, ALU.add).then_inc(s_mean, 1)
                elif kind == "o_b":
                    g = a[0]
                    b = BLOCK_OF[("hg", g)]
                    dve.wait_ge(s_taken[b % 2], taken(b))
                    reciprocal(("o_a", g), inv[:, :], NT * GH)
                    for t in range(NT):
                        ps = bank(USE[("o_a", g, t)])
                        for h in range(GH):
                            cols = slice(h * P, (h + 1) * P)
                            ins = stt(out=E[:, 0, t * GW:(t + 1) * GW][:, cols], in0=ps[:, cols],
                                      scalar=inv[:, GH * t + h:GH * t + h + 1], in1=hgate[:, t, cols],
                                      op0=ALU.mult, op1=ALU.mult)
                        ins.then_inc(s_given["dve"], 1)
                elif kind == "o_t":
                    g, j = a
                    hi, lo, k = (hT_hi, hT_lo, 12 + 2 * j) if g else (mT_hi, mT_lo, 2 * j)
                    split_lo(s, [(lo[:, k:k + 2, :], filled(s)[:, :].rearrange("p (k t) -> p k t", k=2),
                                  hi[:, k:k + 2, :], V_HG)])
                elif kind in ("out1", "out2"):
                    c = a[0]
                    ps, read = block_banks(kind, c)
                    if kind == "out1":
                        dve.wait_ge(s_xagain, 16)
                    else:
                        b = BLOCK_OF[("out1", c)]
                        dve.wait_ge(s_taken[b % 2], taken(b))
                    for t in range(NT):
                        v = X[:, t, c * NB:(c + 1) * NB]
                        tt(v, v, ps[t][:, :], ALU.add).then_inc(read, 1)
                elif kind == "x2":
                    ps, k = filled(s), 4 * a[0] + 2 * a[1]
                    split_lo(s, [(hT_lo[:, k + n, :], ps[:, n * SEQ:(n + 1) * SEQ], hT_hi[:, k + n, :],
                                  V_FFN + k + n) for n in range(2)])

            def multiply_gate(i):
                dve.wait_ge(s_used, G0 + GU + GU * i)
                dve.wait_ge(s_taken[PG], taken(FF) + NT * i)
                for t in range(NT):
                    stt(out=hidden[:, t, :], in0=main[PU][t][:, :], scalar=r_ffn[:, t:t + 1], in1=gate[:, t, :],
                        op0=ALU.mult, op1=ALU.mult).then_inc(s_taken[PU], 1)

            def split_hidden(i):
                for u in range(2):
                    dve.wait_ge(s_ahi, 2 * i + u + 1)
                    at = bass.ds(4 * i + 2 * u, 2)
                    tt(aT_lo[:, at, :], side[u][:, :].rearrange("p (k t) -> p k t", k=2),
                       aT_hi[:, at, :].bitcast(F32), ALU.subtract).then_inc(s_alo, 1)

            def add_down(d):
                b = DOWN + d
                dve.wait_ge(s_used, G1 + DN * (d + 1))
                for t in range(NT):
                    v = X[:, t, d * NB:(d + 1) * NB]
                    tt(v, v, main[b % 2][t][:, :], ALU.add).then_inc(s_taken[b % 2], 1)

            for s in steps_at(-1):
                step(s)
            for g in range(LEAD):
                convert(g % RING, g, granule_size(g))
            for g in range(G0):
                n = g + LEAD
                convert(n % RING, n, granule_size(n))
                for s in steps_at(g):
                    step(s)
            for j in range(GU):
                n = G0 + j + LEAD
                convert(n % RING, n)
                for s in steps_at(G0 + j):
                    step(s)
            with dve.Fori(1, NFF) as i:
                for j in range(GU):
                    n = G0 + j + LEAD
                    convert(n % RING, n + GU * i)
                    if j == 0:
                        multiply_gate(i - 1)
                    if j == 3:
                        split_hidden(i - 1)
            multiply_gate(NFF - 1)
            split_hidden(NFF - 1)
            for j in range(4 * DN):
                n = G1 + j + LEAD
                if n < G1 + 4 * DN:
                    convert(n % RING, n)
                if j and j % DN == 0:
                    add_down(j // DN - 1)
            add_down(3)

        @block.tensor
        def _(pe):
            matmul, transpose = nc.tensor.matmul, nc.tensor.transpose

            def multiply(slot, g, lhs, k_first, k_last, banks, cols, ks):
                hi, lo, at = lhs
                pe.wait_ge(s_hi, g + 1)
                for part in ("hi", "lo"):
                    if part == "lo":
                        pe.wait_ge(s_lo, g + 1)
                    w = w_hi if part == "hi" else w_lo
                    for n, k in enumerate(ks):
                        rhs = w[:, slot, n * cols:(n + 1) * cols]
                        for t in range(NT):
                            tok = slice(t * P, (t + 1) * P)
                            m = matmul(banks[t][:, 0:cols], hi[:, at[n], tok], rhs,
                                       start=(part == "hi" and k == k_first), stop=(part == "lo" and k == k_last))
                            if part == "hi":
                                matmul(banks[t][:, 0:cols], lo[:, at[n], tok], rhs, start=False, stop=False)
                m.then_inc(s_used, 1)

            def use(key):
                n = USE[key]
                if n >= SIDE:
                    pe.wait_ge(s_given[USES[n - SIDE][1]], GIVEN[n - SIDE])
                return bank(n)

            def given(key):
                pe.wait_ge(s_given["act"], GIVEN[USE[key]])

            def turn_x(s, k, where=X):
                ps = use(s)
                for n in range(2):
                    for t in range(NT):
                        at = n * SEQ + t * P
                        m = transpose(ps[:, at:at + P], where[:, t, (k + n) * P:(k + n + 1) * P], ident[:, :])
                m.then_inc(s_side, 1)

            def step(s):
                kind, a = s[0], s[1:]
                if kind == "vec":
                    pe.wait_ge(s_small, 16 * N_SMALL)
                    pe.wait_ge(s_const, N_IDENT)
                    transpose(use(s)[:, 0:V_ROWS], vec_rows[:, :], ident[0:V_ROWS, 0:V_ROWS]).then_inc(s_side, 1)
                elif kind == "x":
                    pe.wait_ge(s_x[a[0] // 2], 16)
                    turn_x(s, 2 * a[0])
                elif kind == "x2":
                    c, j = a
                    b = BLOCK_OF[("out2", c)]
                    pe.wait_ge(s_taken[b % 2], taken(b))
                    turn_x(s, 4 * c + 2 * j)
                elif kind == "lat_t":
                    i, j = a
                    b = BLOCK_OF[("ckv" if i else "cq", 0)]
                    pe.wait_ge(s_taken[b % 2], taken(b))
                    turn_x(s, 2 * j, lat)
                elif kind in ("q_t", "k_t"):
                    j, b = a[0], a[0] % 2
                    pe.wait_ge(s_stage, (0 if kind == "q_t" else HEADS // 2) + j + 1)
                    ps = use(s + (0,))
                    for h in range(2):
                        for t in range(NT):
                            at = h * SEQ + t * P
                            m = transpose(ps[:, at:at + P], stage[:, b, t, h, 0:NOPE], ident[:, :])
                    m.then_inc(s_side, 1)
                    ps = use(s + (1,))
                    for t in range(NT):
                        m = transpose(ps[:, t * P:(t + 1) * P], stage_r[:, b, t, :, :].rearrange("p h r -> p (h r)"),
                                      ident[:, :])
                    m.then_inc(s_side, 1)
                elif kind == "scores":
                    h = a[0]
                    given(("k_t", HEADS // 2 - 1, 1))
                    ps = use(s)
                    part = slice((h % 2) * ROPE, (h % 2 + 1) * ROPE)
                    for t, keys, cols in ((0, slice(0, P), slice(0, P)), (1, slice(0, SEQ), slice(P, 3 * P))):
                        tok = slice(t * P, (t + 1) * P)
                        matmul(ps[:, cols], qTn[:, h, tok], kTn[:, h, keys], start=True, stop=False)
                        m = matmul(ps[:, cols], qTr[part, h // 2, tok], kTr[part, h // 2, keys], start=False, stop=True)
                    m.then_inc(s_side, 1)
                elif kind == "probs_t":
                    h = a[0]
                    pe.wait_ge(s_prob, h + 1)
                    ps = use(s)
                    for n in range(3):
                        cols = slice(n * P, (n + 1) * P)
                        m = transpose(ps[:, cols], probs[:, h % 2, cols], ident[:, :])
                    m.then_inc(s_side, 1)
                elif kind == "attend":
                    h, b = a[0], a[0] % 2
                    given(("probs_t", h))
                    ps = use(s)
                    matmul(ps[:, 0:P], val[:, 0, h, :], probsT[:, b, 0:P], start=True, stop=True)
                    matmul(ps[:, P:SEQ], val[:, 0, h, :], probsT[:, b, P:2 * P], start=True, stop=False)
                    matmul(ps[:, P:SEQ], val[:, 1, h, :], probsT[:, b, 2 * P:3 * P], start=False, stop=True)\
                        .then_inc(s_side, 1)
                elif kind == "turn":
                    g, n, t = a
                    if n == 0:
                        b = BLOCK_OF[("hq", g)]
                        pe.wait_ge(s_taken[b % 2], taken(b))
                    else:
                        pe.wait_ge(s_f if n == 1 else s_logf, g + 1)
                    ps = use(s)
                    for h in range(GH):
                        cols = slice(h * P, (h + 1) * P)
                        if n == 2:
                            m = matmul(ps[:, cols], hlf[:, t, cols], tri[:, :], start=True, stop=True)
                        else:
                            m = transpose(ps[:, cols], (hq, hk)[n][:, t, cols], ident[:, :])
                    m.then_inc(s_side, 1)
                elif kind == "pairs":
                    g, l = a
                    if l == 0:
                        given(("turn", g, 1, NT - 1))
                        left, right = hkT, hqT
                    else:
                        pe.wait_ge(s_lev, (LEVELS + 1) * g + l)
                        left = right = E[:, l % 2, :].rearrange("p (h t) -> p h t", h=GH)
                    for t in range(NT):
                        tok = slice(t * P, (t + 1) * P)
                        ps = use(s + (t,))
                        for h in range(GH):
                            m = matmul(ps[:, h * P:(h + 1) * P], left[:, h, tok], right[:, h, tok], start=True,
                                       stop=True)
                        m.then_inc(s_side, 1)
                elif kind in ("join7", "join8"):
                    g = a[0]
                    ps = use(s)
                    keys, queries = [E[:, n, :].rearrange("p (h t) -> p h t", h=GH) for n in range(2)]
                    if kind == "join7":
                        pe.wait_ge(s_lev, (LEVELS + 1) * (g + 1))
                        for h in range(GH):
                            for t in range(NT):
                                at = (2 * h + t) * CHUNK
                                m = matmul(ps[0:CHUNK, at:at + CHUNK], keys[:, h, t * P:t * P + CHUNK],
                                           queries[:, h, t * P + CHUNK:(t + 1) * P], start=True, stop=True)
                    else:
                        pe.wait_ge(s_join, g + 1)
                        for h in range(GH):
                            m = matmul(ps[:, h * P:(h + 1) * P], keys[:, h, 0:P], queries[:, h, P:SEQ], start=True,
                                       stop=True)
                    m.then_inc(s_side, 1)
                elif kind == "o_a":
                    g = a[0]
                    b = BLOCK_OF[("hi", g)]
                    pe.wait_ge(s_taken[b % 2], taken(b))
                    pe.wait_ge(s_given["dve"], GIVEN[USE[("pairs", g, LEVELS, NT - 1)]])
                    given(("join8", g))
                    for t in range(NT):
                        ps = use(s + (t,))
                        for h in range(GH):
                            cols = slice(h * P, (h + 1) * P)
                            if t:
                                matmul(ps[:, cols], hS[:, h, 2, :], hv[:, 0, cols], start=True, stop=False)
                            m = matmul(ps[:, cols], hS[:, h, t, :], hv[:, t, cols], start=(t == 0), stop=True)
                        m.then_inc(s_side, 1)
                elif kind == "o_t":
                    g, j = a
                    pe.wait_ge(s_given["dve"], GIVEN[USE[("o_a", g, NT - 1)]])
                    turn_x(s, 2 * j, E[:, 0, :].rearrange("p (t c) -> p t c", t=NT))

            def lhs_of(kind, ks):
                if kind == "ukv":
                    return mT_hi, mT_lo, [4 + k for k in ks]
                if kind == "out1":
                    return mT_hi, mT_lo, [(4 + k) % 12 for k in ks]
                if kind == "out2":
                    return hT_hi, hT_lo, [12 + k for k in ks]
                return (mT_hi, mT_lo, ks) if kind == "uq" else (hT_hi, hT_lo, ks)

            for s in steps_at(-1):
                step(s)
            for g, (b, k, n) in enumerate(GRANULES):
                for s in steps_at(g):
                    step(s)
                kind, i, _, _, cols, rows, _ = BLOCKS[b]
                ks = list(range(k, k + n))
                pe.wait_ge(s_tlo, split_needed(g))
                if k == 0 and b >= 2:
                    pe.wait_ge(s_taken[b % 2], taken(b - 2))
                multiply(g % RING, g, lhs_of(kind, ks), 0, len(rows) - 1, main[b % 2], cols, ks)

            def turn_hidden(i):
                pe.wait_ge(s_taken[PU], taken(FF + 1) + NT * i)
                for u in range(2):
                    for n in range(2):
                        for t in range(NT):
                            at = n * SEQ + t * P
                            m = transpose(side[u][:, at:at + P], hidden[:, t, (2 * u + n) * P:(2 * u + n + 1) * P],
                                          ident[:, :])
                    m.then_inc(s_turned, 1)

            def gate_and_up(i, first=False):
                for j in range(GU):
                    g = G0 + j
                    if first:
                        for s in steps_at(g):
                            step(s)
                        pe.wait_ge(s_tlo, SPLIT[("x2",) + divmod(min(j, 7), 2)] + 1)
                    elif j == 3:
                        turn_hidden(i - 1)
                    up = j // (KT // 2)
                    k = 2 * (j % (KT // 2))
                    if k == 0:
                        pe.wait_ge(s_taken[(PG, PU)[up]], taken(FF + up - 2) + NT * i)
                    multiply(g % RING, g + GU * i, (hT_hi, hT_lo, [k, k + 1]), 0, KT - 1, main[(PG, PU)[up]], NB,
                             [k, k + 1])

            gate_and_up(0, True)
            with pe.Fori(1, NFF) as i:
                gate_and_up(i)
            turn_hidden(NFF - 1)
            pe.wait_ge(s_alo, 2 * NFF)
            with pe.Fori(0, 2) as i:
                for j in range(2 * DN):
                    d, k = divmod(j, DN)
                    b = DOWN + d
                    if k == 0:
                        pe.wait_ge(s_taken[b % 2], taken(b - 2) + NT * i)
                    multiply((G1 + j) % RING, G1 + j + 2 * DN * i, (aT_hi, aT_lo, [2 * k, 2 * k + 1]), 0, DOWN_KT - 1,
                             main[b % 2], NB, [2 * k, 2 * k + 1])


def granule_size(g):
    if g >= G0:
        return GRAN
    b, _, n = GRANULES[g]
    return n * BLOCKS[b][4]


_INS = ["x", "positions", "attn_norm_w", "w_in", "hgrn_lb", "hgrn_norm_w", "mla_q_norm_w", "w_uq", "mla_kv_norm_w",
        "w_ukv", "q_head_norm_w", "k_head_norm_w", "w_out", "ffn_norm_w", "w_gate_up", "w_down"]


def kernel(**inputs):
    import concourse.bacc as bacc
    from concourse.bass_utils import run_bass_kernel_spmd

    nc = bacc.Bacc("TRN2", target_bir_lowering=False, num_devices=1)
    arrays, args = {}, []
    for name in _INS:
        a = np.ascontiguousarray(inputs[name])
        arrays[f"in_{name}"] = a
        args.append(nc.dram_tensor(f"in_{name}", a.shape, mybir.dt.from_np(a.dtype), kind="ExternalInput").ap())
    args.append(nc.dram_tensor("out_0", (1, SEQ, D), F32, kind="ExternalOutput").ap())
    hybrid_layer(nc, *args)
    r = run_bass_kernel_spmd(nc, [arrays], core_ids=[0])
    return r.results[0]["out_0"]
```

```python
from contextlib import ExitStack

import numpy as np

import concourse.bass as bass
from concourse import mybir

F32 = mybir.dt.float32
F32R = mybir.dt.float32r
I32 = mybir.dt.int32
ALU = mybir.AluOpType
ACT = mybir.ActivationFunctionType
AX = mybir.AxisListType

P = 128
D = 2048
SEQ = 256
NT = SEQ // P
CHUNK = 64
KT = D // P
HG = 1024
GH = 4
GW = GH * P
LORA = 512
HEADS = 8
NOPE, ROPE = 128, 64
QK = NOPE + ROPE
HALF = ROPE // 2
D_FF = 5632
NB = 512
EPS = 1e-6
SCALE = float(QK) ** -0.5
MASKED = -1e30
LEVELS = 6
RING = 4
LEAD = 3
GRAN = 1024
SIDE = 4

LAT_COLS = (384, 384, 320)
LAT_PIECES = ((0, 0, 384, 0, 0), (1, 0, 128, 0, 384), (1, 128, 256, 1, 0), (2, 0, 256, 1, 256), (2, 256, ROPE, 2, 0))

V_ATTN, V_FFN, V_QN, V_KVN, V_HG, V_ROWS = 0, KT, 2 * KT, 2 * KT + 4, 2 * KT + 8, 2 * KT + 9


ORDER = "hq0 uq0 hf0 ukv0 hi0 uq1 hg0 ukv1 hq1 uq2 ukv2 hf1 uq3 ukv3 hi1 hg1"


def main_blocks():
    def rows(n, first=0):
        return [first + P * k for k in range(n)]
    w, at = [], 4 * HG
    for n, cols in enumerate(LAT_COLS):
        w.append(("lat", n, "w_in", at, cols, rows(KT), 2))
        at += cols
    first = {"hq": 0, "hf": HG, "hi": 2 * HG, "hg": 3 * HG}
    for name in ORDER.split():
        kind, n = name[:-1], int(name[-1])
        if kind == "uq":
            w.append((kind, n, "w_uq", 2 * QK * n, 2 * QK, rows(LORA // P), 2))
        elif kind == "ukv":
            w.append((kind, n, "w_ukv", NB * n, NB, rows(LORA // P), 2))
        else:
            w.append((kind, n, "w_in", first[kind] + GW * n, GW, rows(KT), 2))
    w += [("out1", c, "w_out", NB * c, NB, rows(8, HG) + rows(4), 2) for c in range(4)]
    w += [("out2", c, "w_out", NB * c, NB, rows(4, GW), 2) for c in range(4)]
    return w


BLOCKS = main_blocks()
GRANULES = [(b, k, blk[6]) for b, blk in enumerate(BLOCKS) for k in range(0, len(blk[5]), blk[6])]
G0 = len(GRANULES)
END = {blk[:2]: 1 + max(g for g, x in enumerate(GRANULES) if x[0] == b) for b, blk in enumerate(BLOCKS)}
BLOCK_OF = {blk[:2]: b for b, blk in enumerate(BLOCKS)}
NFF = D_FF // NB
GU = 2 * KT // 2
DOWN_KT = D_FF // P
DN = DOWN_KT // 2
G1 = G0 + NFF * GU


FIRST = -LEAD - 1


def schedule():
    s = [(FIRST, ("vec", 0)), (FIRST, ("x", 0)), (-2, ("x", 1))] + [(j - 2, ("x", j)) for j in range(2, 8)]
    s += [(2 * c + 1, ("sq1", c)) for c in range(4)]
    s += [(8, ("r1a",)), (9, ("r1b",)), (18, ("vec", 1))]
    s += [(END[("lat", n)] + 2 * (n == 0), ("lat_in", n)) for n in range(3)]
    for i in range(2):
        e = END[("lat", i + 1)]
        s += [(e + 1, ("lat_a", i)), (e + 2, ("lat_b", i))] + [(e + 5, ("lat_t", i, n)) for n in range(2)]
    e = END[("lat", 2)]
    s += [(e + 1, ("kr_a",)), (e + 4, ("angles",)), (e + 5, ("sines",)), (e + 9, ("kr_b",))]
    s += [(e + 7, ("lb_a", 0)), (e + 13, ("lb_b", 0)), (e + 15, ("lb_c", 0))]
    e = END[("ukv", 2)]
    s += [(e + 2, ("lb_a", 1)), (e + 3, ("lb_b", 1)), (e + 5, ("lb_c", 1))]
    for j in range(HEADS // 2):
        q, k = END[("uq", j)], END[("ukv", j)]
        early = j >= 2
        s += [(q - early, ("q_a", j)), (q - 1 if early else q + 1, ("q_b", j)), (q + 4, ("q_t", j))]
        early = j == 2
        s += [(k - early, ("k_a", j)), (k - 1 if early else k + 1, ("k_b", j)), (k + 4, ("k_t", j))]
        for h in (2 * j, 2 * j + 1):
            p = k + 5 + (j > 1) + (7 if j == 2 else 3) * (h % 2)
            s += [(p, ("scores", h)), (p + 1, ("softmax", h)), (p + 3, ("probs_t", h)),
                  (p + 5 + (h == 4), ("attend", h))]
    for g in range(2):
        late = 5 * g
        e = END[("hf", g)]
        s += [(END[("hq", g)], ("hq", g)), (e - g, ("hf_a", g)), (e + 2 + late, ("hf_b", g))]
        s += [(e + 2 + 2 * g + n, ("turn", g, n, t)) for n in range(2) for t in range(NT)]
        s += [(e + 4 + late, ("turn", g, 2, t)) for t in range(NT)]
        p = e + 6 + late
        s += [(p, ("pairs", g, 0))]
        for l in range(1, LEVELS + 1):
            s += [(p, ("lev_a", g, l)), (p + 1, ("lev_b", g, l)), (p + 4, ("pairs", g, l))]
            p += 3
        s += [(p + 1, ("join_a", g)), (p + 2, ("join_b", g)), (p + 5, ("join7", g)), (p + 6, ("join_c", g)),
              (p + 8, ("join8", g))]
        s += [(END[("hi", g)], ("hi", g)), (END[("hg", g)], ("hg", g))]
        p = max(p + 10, END[("hg", g)] + 2, END[("ukv", 2)] + 3)
        s += [(p, ("o_a", g)), (p + 1, ("o_b", g))]
        p = max(p + 4 - g, END[("ukv", HEADS // 2 - 1)] + 6)
        s += [(p, ("o_t", g, 0)), (p, ("o_t", g, 1))]
    for c in range(4):
        s += [(END[("out1", c)], ("out1", c)), (END[("out2", c)], ("out2", c)), (END[("out2", c)] + 1, ("sq2", c))]
    s += [(END[("out2", c)] + 2, ("x2", c, n)) for c in range(4) for n in range(2)]
    e = END[("out2", 3)]
    s += [(e + 3, ("r2a",)), (e + 4, ("r2b",))]
    return sorted(s, key=lambda x: x[0])


SCHEDULE = schedule()
MT = [(k + 8) % 12 for k in range(12)]


def loads(g):
    return g // RING + 1


def steps_at(position):
    return [step for p, step in SCHEDULE if p == position]


def side_uses(step):
    kind = step[0]
    if kind in ("x", "x2", "lat_t", "o_t"):
        return [(step, "dve")]
    if kind in ("vec", "turn", "probs_t", "join7", "join8"):
        return [(step, "act")]
    if kind in ("q_t", "k_t"):
        return [(step + (0,), "act"), (step + (1,), "act")]
    if kind == "pairs" and step[2]:
        return [(step, "dve")]
    if kind in ("pairs", "o_a"):
        return [(step + (t,), "dve") for t in range(NT)]
    if kind in ("scores", "attend"):
        return [(step, "dve")]
    return []


USES = [u for _, step in SCHEDULE for u in side_uses(step)]
USE = {key: n for n, (key, _) in enumerate(USES)}
GIVEN, _given = {}, {"act": 0, "dve": 0}
for _, _step in SCHEDULE:
    if _step[0] != "o_a":
        for _key, _engine in side_uses(("o_a", _step[1]) if _step[0] == "o_b" else _step):
            _given[_engine] += 1
            GIVEN[USE[_key]] = _given[_engine]
SPLITS = [step for _, step in SCHEDULE if step[0] in ("x", "x2", "lat_t", "o_t", "attend")]
SPLIT = {step: n for n, step in enumerate(SPLITS)}
RMS = [step for _, step in SCHEDULE if step[0] in ("r1a", "lat_a", "q_a", "k_a", "o_a", "r2a")]


def squares_of(step):
    return {"sq1": NT, "lat_a": 2, "kr_a": 2, "q_a": 4, "k_a": 4, "o_a": NT * GH, "sq2": NT}.get(step[0], 0)


SQUARES = {}
for _, _step in SCHEDULE:
    SQUARES[_step] = sum(squares_of(s) for s in SQUARES) + squares_of(_step)


def split_needed(g):
    b, k, n = GRANULES[g]
    kind, i = BLOCKS[b][:2]
    if (kind, i) == ("lat", 0):
        return SPLIT[("x", k // 2)] + 1
    if kind == "uq":
        return SPLIT[("lat_t", 0, 1)] + 1
    if kind == "ukv":
        return SPLIT[("lat_t", 1, 1)] + 1
    if kind == "out1":
        return max(SPLIT[("attend", HEADS - 1)], SPLIT[("o_t", 0, 1)]) + 1
    if kind == "out2":
        return SPLIT[("o_t", 1, 1)] + 1
    return SPLIT[("x", 7)] + 1


def hybrid_layer(nc, x, positions, attn_norm_w, w_in, hgrn_lb, hgrn_norm_w, mla_q_norm_w, w_uq, mla_kv_norm_w,
                 w_ukv, q_head_norm_w, k_head_norm_w, w_out, ffn_norm_w, w_gate_up, w_down, out):
    weights = {"w_in": w_in[0], "w_uq": w_uq[0], "w_ukv": w_ukv[0], "w_out": w_out[0]}
    w_gu = w_gate_up[0]
    w_dn = w_down[0]
    x_v = x[0].rearrange("(t p) d -> p t d", p=P)
    out_v = out[0].rearrange("(t p) d -> p t d", p=P)

    with ExitStack() as ctx:
        def sb(name, shape, dt=F32, where=ctx):
            return where.enter_context(nc.sbuf_tensor(name, shape, dt))

        def sem(name):
            return ctx.enter_context(nc.semaphore(name))

        raw = sb("raw", [P, RING, GRAN])
        w_hi = sb("w_hi", [P, RING, GRAN], F32R)
        w_lo = sb("w_lo", [P, RING, GRAN], F32R)
        hT_hi = sb("hT_hi", [P, KT, SEQ], F32R)
        hT_lo = sb("hT_lo", [P, KT, SEQ], F32R)
        X = sb("X", [P, NT, D])
        ident = sb("ident", [P, P])
        vec_cols = sb("vec_cols", [P, V_ROWS])
        junk = sb("junk", [P, QK])
        stat = sb("stat", [P, 72])
        r_in = stat[:, 0:2]
        r_ffn = stat[:, 2:4]
        sumsq = stat[:, 4:12]
        std = stat[:, 12:20]
        inv = stat[:, 20:28]
        sumsq_kr = stat[:, 28:30]
        top = stat[:, 30:34]
        shift = stat[:, 34:38]
        total_p = stat[:, 38:42]
        inv_p = stat[:, 42:46]
        sumsq_x = stat[:, 46:54]
        guess = stat[:, 54:62]
        polish = stat[:, 62:70]

        mix = ctx.enter_context(ExitStack())

        def mb(name, shape, dt=F32):
            return sb(name, shape, dt, mix)

        mT_hi = mb("mT_hi", [P, 12, SEQ], F32R)
        mT_lo = mb("mT_lo", [P, 12, SEQ], F32R)
        lat = mb("lat", [P, NT, LORA])
        stage = mb("stage", [P, 2, NT, 2, QK])
        stage_r = mb("stage_r", [P, 2, NT, 2, ROPE])
        rot = mb("rot", [P, 4, NT, 2, HALF])
        qTr = mb("qTr", [P, HEADS // 2, SEQ])
        kTr = mb("kTr", [P, HEADS // 2, SEQ])
        val = mb("val", [P, NT, HEADS, P])
        kr = mb("kr", [P, NT, ROPE])
        krw = mb("krw", [P, NT, ROPE])
        probs = mb("probs", [P, 2, 3 * P])
        probsT = mb("probsT", [P, 2, 3 * P])
        mask_add = mb("mask_add", [P, 2 * P])
        qw_row = mb("qw_row", [P, QK])
        kw_row = mb("kw_row", [P, QK])
        pos_i = mb("pos_i", [P, NT], I32)
        pos_f = mb("pos_f", [P, NT])
        freq = mb("freq", [P, HALF])
        sincos = mb("sincos", [P, 2, NT, HALF])
        turns = rot[:, 0, :, :, :]
        turns_hi = rot[:, 1, :, :, :]
        vec_rows = stage[0:KT, 0, 0, 0, 0:P]
        more_rows = stage[0:V_ROWS - KT, 0, 0, 1, 0:P]
        tri = mb("tri", [P, P])
        masks = mb("masks", [P, LEVELS, P])
        hq = lat
        hk = mb("hk", [P, NT, GW])
        hlf = mb("hlf", [P, NT, GW])
        hv = mb("hv", [P, NT, GW])
        hgate = mb("hgate", [P, NT, GW])
        hqT = mb("hqT", [P, GH, SEQ])
        hkT = mb("hkT", [P, GH, SEQ])
        hbT = mb("hbT", [P, GH, SEQ])
        E = mb("E", [P, 2, GH * SEQ])
        lb = E[:, 1, :].rearrange("p (n c) -> p n c", n=2)
        lb_tmp = hk[:, 0, :]
        wide_junk = hlf[:, 0, :]
        chunk_decay = mb("chunk_decay", [P, GH, SEQ // CHUNK])
        hS = mb("hS", [P, GH, 3, P])
        latents = (lat, hv)
        qTn = X[:, 0, :].rearrange("p (h t) -> p h t", h=HEADS)
        kTn = X[:, 1, :].rearrange("p (h t) -> p h t", h=HEADS)
        mix.close()

        aT_hi = sb("aT_hi", [P, DOWN_KT, SEQ], F32R)
        aT_lo = sb("aT_lo", [P, DOWN_KT, SEQ], F32R)
        gate = sb("gate", [P, NT, NB])
        hidden = sb("hidden", [P, NT, NB])

        main = [[ctx.enter_context(nc.psum_tensor(f"main{p}{t}", [P, NB], F32)) for t in range(NT)] for p in range(2)]
        side = [ctx.enter_context(nc.psum_tensor(f"side{n}", [P, NB], F32)) for n in range(SIDE)]

        s_raw = [sem(f"s_raw{i}") for i in range(RING)]
        s_hi = sem("s_hi")
        s_lo = sem("s_lo")
        s_used = sem("s_used")
        s_taken = [sem(f"s_taken{p}") for p in range(2)]
        s_side = sem("s_side")
        s_given = {"act": sem("s_given_act"), "dve": sem("s_given_dve")}
        s_thi = sem("s_thi")
        s_tlo = sem("s_tlo")
        s_x = [sem(f"s_x{c}") for c in range(8)]
        s_attn = sem("s_attn")
        s_small = sem("s_small")
        s_lbin = sem("s_lbin")
        s_lbused = sem("s_lbused")
        s_xagain = sem("s_xagain")
        s_const = sem("s_const")
        s_dchain = sem("s_dchain")
        s_lat = sem("s_lat")
        s_sq = sem("s_sq")
        s_mean = sem("s_mean")
        s_std = sem("s_std")
        s_inv = sem("s_inv")
        s_angle = sem("s_angle")
        s_sin = sem("s_sin")
        s_lbmax = sem("s_lbmax")
        s_lbexp = sem("s_lbexp")
        s_stage = sem("s_stage")
        s_val = sem("s_val")
        s_top = sem("s_top")
        s_exp = sem("s_exp")
        s_prob = sem("s_prob")
        s_f = sem("s_f")
        s_logf = sem("s_logf")
        s_arg = sem("s_arg")
        s_dec = sem("s_dec")
        s_lev = sem("s_lev")
        s_join = sem("s_join")
        s_turned = sem("s_turned")
        s_ahi = sem("s_ahi")
        s_alo = sem("s_alo")
        s_out = sem("s_out")

        block = ctx.enter_context(nc.Block())

        FF = len(BLOCKS)
        DOWN = FF + 2 * NFF
        PG, PU = FF % 2, (FF + 1) % 2

        def taken(b):
            return NT * (b // 2 + 1)

        def bank(n):
            return side[n % SIDE]

        small_loads = [(more_rows[r - KT:r - KT + w.shape[1] // P, :], w.rearrange("a (k p) -> (a k) p", p=P))
                       for r, w in ((V_FFN, ffn_norm_w), (V_QN, mla_q_norm_w), (V_KVN, mla_kv_norm_w),
                                    (V_HG, hgrn_norm_w))]
        small_loads += [(pos_i[:, :], positions[0].rearrange("(t p) -> p t", p=P)),
                        (qw_row[:, :], q_head_norm_w[0].partition_broadcast(P)),
                        (kw_row[:, :], k_head_norm_w[0].partition_broadcast(P))]
        N_SMALL = len(small_loads)
        N_IDENT = 2
        N_CONST = 2 + 3 + 1 + 3 * LEVELS + 1 + 2 + HALF

        @block.sync
        def _(sp):
            def slot_free(g):
                sp.wait_ge(s_hi, g - RING + 1)
                sp.wait_ge(s_lo, g - RING + 1)

            def load_x(n):
                cols = slice(2 * P * n, 2 * P * (n + 1))
                sp.dma_start(X[:, :, cols], x_v[:, :, cols]).then_inc(s_x[n], 16)

            sp.dma_start(vec_rows[0:KT, :], attn_norm_w.rearrange("a (k p) -> (a k) p", p=P)).then_inc(s_attn, 16)
            load_x(0)
            for g, (b, k, n) in enumerate(GRANULES):
                kind, i, w, c0, cols, rows, _ = BLOCKS[b]
                if g >= RING:
                    slot_free(g)
                src = weights[w][rows[k]:rows[k] + n * P, c0:c0 + cols].rearrange("(k p) c -> p k c", p=P)
                dst = raw[:, g % RING, 0:n * cols].rearrange("p (k c) -> p k c", k=n)
                sp.dma_start(dst, src).then_inc(s_raw[g % RING], 16)
                for c in ((1, 2) if g == 0 else (g + 2,)):
                    if c < len(s_x):
                        load_x(c)
                if 0 <= g - 7 < N_SMALL:
                    dst, src = small_loads[g - 7]
                    sp.dma_start(dst, src, allow_slow_non_contiguous=True).then_inc(s_small, 16)
            with sp.Fori(0, NFF) as i:
                for half in range(2):
                    for k in range(KT // 2):
                        j = half * (KT // 2) + k
                        slot = (G0 + j) % RING
                        slot_free(G0 + j + GU * i)
                        src = w_gu[2 * P * k:2 * P * (k + 1), bass.ds(half * D_FF + NB * i, NB)]
                        sp.dma_start(raw[:, slot, :].rearrange("p (k c) -> p k c", k=2),
                                     src.rearrange("(k p) c -> p k c", p=P)).then_inc(s_raw[slot], 16)
            with sp.Fori(0, 2) as i:
                for j in range(2 * DN):
                    slot = (G1 + j) % RING
                    slot_free(G1 + j + 2 * DN * i)
                    k = j % DN
                    src = w_dn[2 * P * k:2 * P * (k + 1), bass.ds(NB * (j // DN) + 2 * NB * i, NB)]
                    sp.dma_start(raw[:, slot, :].rearrange("p (k c) -> p k c", k=2),
                                 src.rearrange("(k p) c -> p k c", p=P)).then_inc(s_raw[slot], 16)
            for d in range(3):
                sp.wait_ge(s_taken[(DOWN + d) % 2], taken(DOWN + d))
                cols = slice(d * NB, (d + 1) * NB)
                sp.dma_start(out_v[:, :, cols], X[:, :, cols]).then_inc(s_out, 16)
            for t in range(NT):
                sp.wait_ge(s_taken[(DOWN + 3) % 2], taken(DOWN + 3) - NT + t + 1)
                sp.dma_start(out_v[:, t, 3 * NB:], X[:, t, 3 * NB:]).then_inc(s_out, 16)
            sp.wait_ge(s_out, (3 + NT) * 16)

        @block.gpsimd
        def _(pool):
            made = [0]

            def done(ins):
                made[0] += 1
                ins.then_inc(s_const, 1)

            def settle():
                pool.wait_ge(s_const, made[0])

            done(pool.memset(ident[:, :], 0.0))
            settle()
            done(pool.affine_select(out=ident[:, :], in_=ident[:, :], compare_op=ALU.not_equal, fill=1.0, base=0,
                                    pattern=[[-1, P]], channel_multiplier=1))
            pool.dma_start(lb[:, :, :], hgrn_lb[:, 0:GW].partition_broadcast(P)).then_inc(s_lbin, 16)
            done(pool.memset(mask_add[:, :], 0.0))
            settle()
            done(pool.memset(mask_add[0:CHUNK, 2 * P - CHUNK:2 * P], MASKED))
            for n in range(HALF):
                f = np.float32(1.0) / np.power(np.float32(10000.0), np.float32(2 * n) / np.float32(ROPE))
                done(pool.memset(freq[:, n:n + 1], float(f)))
            v = tri[:, :].rearrange("p (c t) -> p c t", c=2)
            done(pool.memset(tri[:, :], 1.0))
            settle()
            done(pool.affine_select(out=v, in_=v, compare_op=ALU.is_ge, fill=0.0, base=0,
                                    pattern=[[CHUNK, 2], [1, CHUNK]], channel_multiplier=-1))
            settle()
            done(pool.affine_select(out=v, in_=v, compare_op=ALU.is_ge, fill=0.0, base=0,
                                    pattern=[[-CHUNK, 2], [0, CHUNK]], channel_multiplier=1))
            done(pool.memset(masks[:, :, :], 0.0))
            settle()
            for l in range(1, LEVELS + 1):
                h = 1 << (l - 1)
                n = P // (2 * h)
                v = masks[:, l - 1, :].rearrange("p (n two h) -> p n two h", two=2, h=h)[:, :, 1, :]
                done(pool.memset(v, 1.0))
                settle()
                done(pool.affine_select(out=v, in_=v, compare_op=ALU.is_ge, fill=0.0, base=0,
                                        pattern=[[-2 * h, n], [0, h]], channel_multiplier=1))
                settle()
                done(pool.affine_select(out=v, in_=v, compare_op=ALU.is_ge, fill=0.0, base=h - 1,
                                        pattern=[[2 * h, n], [0, h]], channel_multiplier=-1))
            done(pool.memset(hS[:, :, :, :], 0.0))
            pool.wait_ge(s_lbused, 1)
            pool.wait_ge(s_side, USE[("join8", 0)] + 1)
            pool.dma_start(lb[:, :, :], hgrn_lb[:, GW:2 * GW].partition_broadcast(P)).then_inc(s_lbin, 16)
            pool.wait_ge(s_side, USE[("scores", HEADS - 1)] + 1)
            pool.dma_start(X[:, :, :], x_v).then_inc(s_xagain, 16)

        @block.scalar
        def _(act):
            activation = nc.scalar.activation
            copy = nc.scalar.copy

            def convert(slot, load, g, n=GRAN):
                act.wait_ge(s_raw[slot], 16 * load)
                if not isinstance(g, int) or g >= RING:
                    act.wait_ge(s_used, g - RING + 1)
                copy(w_hi[:, slot, 0:n], raw[:, slot, 0:n]).then_inc(s_hi, 1)

            def block_banks(kind, i):
                act.wait_ge(s_used, END[(kind, i)])
                b = BLOCK_OF[(kind, i)]
                return main[b % 2], s_taken[b % 2]

            def filled(key):
                act.wait_ge(s_side, USE[key] + 1)
                return bank(USE[key])

            n_squares = [0]

            def square(src, total, **kw):
                if n_squares[0]:
                    act.wait_ge(s_sq, n_squares[0])
                n_squares[0] += 1
                n = src.shape[-1]
                dst = junk if n <= QK else wide_junk
                activation(dst[:, 0:n], src, ACT.Square, accum_out=total, **kw).then_inc(s_sq, 1)

            def sums_free(step):
                if RMS.index(step):
                    act.wait_ge(s_mean, RMS.index(step))

            def root(step, n):
                i = RMS.index(step)
                act.wait_ge(s_mean, i + 1)
                activation(guess[:, 0:n], std[:, 0:n], ACT.Ln).then_inc(s_std, 1)
                act.wait_ge(s_std, 2 * i + 1)
                activation(guess[:, 0:n], guess[:, 0:n], ACT.Exp, scale=-0.5).then_inc(s_std, 1)

            def table(name="natural_log_exp_and_others"):
                nc.scalar.preload_act_table_set(name)

            def split_hi(parts):
                for dst, src, col in parts:
                    if col is None:
                        ins = copy(dst, src)
                    else:
                        ins = activation(dst, src, ACT.Copy, scale=vec_cols[:, col:col + 1])
                ins.then_inc(s_thi, 1)

            def step(s):
                kind, a = s[0], s[1:]
                if kind == "vec":
                    lo, hi = ((0, KT), (KT, V_ROWS))[a[0]]
                    copy(vec_cols[:, lo:hi], filled(s)[:, 0:hi - lo]).then_inc(s_given["act"], 1)
                    act.wait_ge(s_given["act"], GIVEN[USE[s]])
                elif kind == "x":
                    ps, k = filled(s), 2 * a[0]
                    split_hi([(hT_hi[:, k + n, :], ps[:, n * SEQ:(n + 1) * SEQ], V_ATTN + k + n) for n in range(2)])
                elif kind == "sq1":
                    c = a[0]
                    for n in (2 * c, 2 * c + 1):
                        act.wait_ge(s_x[n], 16)
                    for t in range(NT):
                        square(X[:, t, c * NB:(c + 1) * NB], sumsq[:, 4 * t + c:4 * t + c + 1])
                elif kind == "r1b":
                    root(("r1a",), NT)
                elif kind == "sines":
                    act.wait_ge(s_angle, 1)
                    activation(sincos[:, :, :, :], sincos[:, :, :, :], ACT.Sin).then_inc(s_sin, 1)
                    table()
                elif kind == "lat_a":
                    i = a[0]
                    b = BLOCK_OF[("lat", i + 1)]
                    act.wait_ge(s_taken[b % 2], taken(b))
                    sums_free(s)
                    for t in range(NT):
                        square(latents[i][:, t, :], sumsq[:, t:t + 1])
                elif kind == "lat_b":
                    root(("lat_a",) + a, NT)
                elif kind == "lat_t":
                    i, j = a
                    ps, k, col = filled(s), 4 * i + 2 * j, (V_KVN if i else V_QN) + 2 * j
                    split_hi([(mT_hi[:, k + n, :], ps[:, n * SEQ:(n + 1) * SEQ], col + n) for n in range(2)])
                elif kind == "kr_a":
                    for t in range(NT):
                        square(krw[:, t, :], sumsq_kr[:, t:t + 1])
                elif kind == "lb_b":
                    act.wait_ge(s_lbmax, a[0] + 1)
                    activation(lb[:, :, :], lb[:, :, :], ACT.Exp).then_inc(s_lbexp, 1)
                elif kind in ("q_a", "k_a"):
                    ps, _ = block_banks("uq" if kind == "q_a" else "ukv", a[0])
                    width, stride = (QK, QK) if kind == "q_a" else (NOPE, NOPE + P)
                    sums_free(s)
                    for t in range(NT):
                        for h in range(2):
                            square(ps[t][:, h * stride:h * stride + width], sumsq[:, 2 * t + h:2 * t + h + 1])
                elif kind in ("q_b", "k_b"):
                    root((kind[0] + "_a",) + a, 2 * NT)
                    if kind == "k_b":
                        ps, _ = block_banks("ukv", a[0])
                        for t in range(NT):
                            src = ps[t][:, :].rearrange("p (h c) -> p h c", h=2)[:, :, NOPE:NOPE + P]
                            copy(val[:, t, 2 * a[0]:2 * a[0] + 2, :], src).then_inc(s_val, 1)
                elif kind in ("q_t", "k_t"):
                    j = a[0]
                    plain, rotated = (qTn, qTr) if kind == "q_t" else (kTn, kTr)
                    copy(plain[:, 2 * j:2 * j + 2, :], filled(s + (0,))[:, :].rearrange("p (h t) -> p h t", h=2))\
                        .then_inc(s_given["act"], 1)
                    copy(rotated[:, j, :], filled(s + (1,))[:, 0:SEQ]).then_inc(s_given["act"], 1)
                elif kind == "softmax":
                    h, b = a[0], a[0] % 2
                    act.wait_ge(s_top, h + 1)
                    for t, (lo, hi) in enumerate(((0, P), (P, 3 * P))):
                        activation(probs[:, b, lo:hi], probs[:, b, lo:hi], ACT.Exp, scale=SCALE,
                                   bias=shift[:, 2 * b + t:2 * b + t + 1],
                                   accum_out=total_p[:, 2 * b + t:2 * b + t + 1]).then_inc(s_exp, 1)
                elif kind == "probs_t":
                    copy(probsT[:, a[0] % 2, :], filled(s)[:, 0:3 * P]).then_inc(s_given["act"], 1)
                elif kind == "attend":
                    split_hi([(mT_hi[:, MT[a[0]], :], filled(s)[:, 0:SEQ], None)])
                elif kind in ("hq", "hf_a", "hi", "hg"):
                    ps, read = block_banks(kind[:2], a[0])
                    dst, fn = {"hq": (hq, ACT.Silu), "hf_a": (hlf, ACT.Sigmoid), "hi": (hv, ACT.Copy),
                               "hg": (hgate, ACT.Silu)}[kind]
                    if kind == "hq" and not a[0]:
                        act.wait_ge(s_side, USE[("lat_t", 0, 1)] + 1)
                    if a[0] and kind == "hg":
                        act.wait_ge(s_given["dve"], GIVEN[USE[("o_a", 0, NT - 1)]])
                    for t in range(NT):
                        activation(dst[:, t, :], ps[t][:, :], fn, scale=r_in[:, t:t + 1]).then_inc(read, 1)
                    table("natural_log" if s == ("hf_a", 0) else "natural_log_exp_and_others")
                elif kind == "hf_b":
                    if a[0]:
                        table("natural_log")
                    act.wait_ge(s_f, a[0] + 1)
                    activation(hlf[:, :, :], hlf[:, :, :], ACT.Ln).then_inc(s_logf, 1)
                    table()
                elif kind == "turn":
                    g, n, t = a
                    if g:
                        act.wait_ge(s_join, g)
                    copy((hqT, hkT, hbT)[n][:, :, t * P:(t + 1) * P],
                         filled(s)[:, :].rearrange("p (h t) -> p h t", h=GH)).then_inc(s_given["act"], 1)
                elif kind == "lev_b":
                    g, l = a
                    act.wait_ge(s_arg, (LEVELS + 1) * g + l)
                    v = E[:, l % 2, :].rearrange("p (n two h) -> p n two h", two=2, h=1 << (l - 1))
                    activation(v[:, :, 0, :], v[:, :, 0, :], ACT.Exp, scale=-1.0)
                    activation(v[:, :, 1, :], v[:, :, 1, :], ACT.Exp).then_inc(s_dec, 1)
                elif kind == "join_b":
                    act.wait_ge(s_arg, (LEVELS + 1) * (a[0] + 1))
                    activation(E[:, 0, :], E[:, 0, :], ACT.Exp, scale=-1.0)
                    activation(E[:, 1, :], hbT[:, :, :].rearrange("p h t -> p (h t)"), ACT.Exp)
                    ends = hbT[:, :, :].rearrange("p h (c t) -> p h c t", t=CHUNK)[:, :, :, CHUNK - 1]
                    activation(chunk_decay[:, :, :], ends, ACT.Exp).then_inc(s_dec, 1)
                elif kind == "join7":
                    src = filled(s)[0:CHUNK, :].rearrange("p (h t c) -> p h t c", h=GH, t=2)
                    copy(hS[0:CHUNK, :, 0:2, CHUNK:P], src).then_inc(s_given["act"], 1)
                elif kind == "join8":
                    copy(hS[:, :, 2, :], filled(s)[:, :].rearrange("p (h t) -> p h t", h=GH))\
                        .then_inc(s_given["act"], 1)
                elif kind == "o_a":
                    sums_free(s)
                    for t in range(NT):
                        ps = filled(s + (t,))
                        for h in range(GH):
                            square(ps[:, h * P:(h + 1) * P], sumsq[:, GH * t + h:GH * t + h + 1])
                elif kind == "o_b":
                    root(("o_a",) + a, NT * GH)
                elif kind == "o_t":
                    g, j = a
                    dst, k = (hT_hi, 12 + 2 * j) if g else (mT_hi, MT[HEADS + 2 * j])
                    split_hi([(dst[:, k:k + 2, :], filled(s)[:, :].rearrange("p (k t) -> p k t", k=2), V_HG)])
                elif kind == "sq2":
                    c = a[0]
                    b = BLOCK_OF[("out2", c)]
                    act.wait_ge(s_taken[b % 2], taken(b))
                    for t in range(NT):
                        square(X[:, t, c * NB:(c + 1) * NB], sumsq_x[:, 4 * t + c:4 * t + c + 1])
                elif kind == "x2":
                    ps, k = filled(s), 4 * a[0] + 2 * a[1]
                    split_hi([(hT_hi[:, k + n, :], ps[:, n * SEQ:(n + 1) * SEQ], V_FFN + k + n) for n in range(2)])
                elif kind == "r2b":
                    root(("r2a",), NT)

            def silu(i):
                act.wait_ge(s_used, G0 + KT // 2 + GU * i)
                for t in range(NT):
                    activation(gate[:, t, :], main[PG][t][:, :], ACT.Silu, scale=r_ffn[:, t:t + 1])\
                        .then_inc(s_taken[PG], 1)

            def split_hidden(i):
                for u in range(2):
                    act.wait_ge(s_turned, 2 * i + u + 1)
                    copy(aT_hi[:, bass.ds(4 * i + 2 * u, 2), :],
                         side[u][:, :].rearrange("p (k t) -> p k t", k=2)).then_inc(s_ahi, 1)

            table("natural_log_exp_and_others")
            for g in range(FIRST, G0):
                n = g + LEAD
                if n >= 0:
                    convert(n % RING, loads(n), n, granule_size(n))
                for s in steps_at(g):
                    step(s)
            for j in range(GU):
                n = G0 + j + LEAD
                convert(n % RING, loads(n), n)
                for s in steps_at(G0 + j):
                    step(s)
                if j == KT // 2:
                    act.wait_ge(s_inv, len(RMS))
                    silu(0)
            with act.Fori(1, NFF) as i:
                for j in range(GU):
                    n = G0 + j + LEAD
                    convert(n % RING, loads(n) + (GU // RING) * i, n + GU * i)
                    if j == 3:
                        split_hidden(i - 1)
                    if j == KT // 2:
                        act.wait_ge(s_taken[PU], taken(FF + 1) + NT * (i - 1))
                        silu(i)
            split_hidden(NFF - 1)
            for n in range(G1 + LEAD, G1 + 4 * DN):
                convert(n % RING, loads(n), n)

        @block.vector
        def _(dve):
            tt, ts, stt = nc.vector.tensor_tensor, nc.vector.tensor_scalar, nc.vector.scalar_tensor_tensor
            chain = [0]

            def link(ins):
                chain[0] += 1
                ins.then_inc(s_dchain, 1)
                dve.wait_ge(s_dchain, chain[0])

            def convert(slot, g, n=GRAN):
                dve.wait_ge(s_hi, g + 1)
                tt(w_lo[:, slot, 0:n], raw[:, slot, 0:n], w_hi[:, slot, 0:n].bitcast(F32), ALU.subtract)\
                    .then_inc(s_lo, 1)

            def block_banks(kind, i):
                dve.wait_ge(s_used, END[(kind, i)])
                b = BLOCK_OF[(kind, i)]
                return main[b % 2], s_taken[b % 2]

            def filled(key):
                dve.wait_ge(s_side, USE[key] + 1)
                return bank(USE[key])

            def split_lo(s, parts):
                dve.wait_ge(s_thi, SPLIT[s] + 1)
                for dst, src, hi, col in parts:
                    if col is None:
                        ins = tt(dst, src, hi.bitcast(F32), ALU.subtract)
                    else:
                        ins = stt(out=dst, in0=src, scalar=vec_cols[:, col:col + 1], in1=hi.bitcast(F32),
                                  op0=ALU.mult, op1=ALU.subtract)
                ins.then_inc(s_tlo, 1)
                dve.wait_ge(s_tlo, SPLIT[s] + 1)
                dve.sem_inc(s_given["dve"], 1)

            def mean(n, width):
                ts(std[:, 0:n], std[:, 0:n], 1.0 / width, EPS, ALU.mult, ALU.add).then_inc(s_mean, 1)

            def sums(s):
                dve.wait_ge(s_sq, SQUARES[s])

            def reciprocal(s, dst, n):
                dve.wait_ge(s_std, 2 * (RMS.index(s) + 1))
                y, e = guess[:, 0:n], polish[:, 0:n]
                link(tt(e, y, y, ALU.mult))
                link(stt(out=e, in0=e, scalar=-0.5, in1=std[:, 0:n], op0=ALU.mult, op1=ALU.mult))
                stt(out=dst, in0=e, scalar=1.5, in1=y, op0=ALU.add, op1=ALU.mult).then_inc(s_inv, 1)
                dve.wait_ge(s_inv, RMS.index(s) + 1)

            def rotate(dst, src):
                n = src.shape[2]
                a, b = src[:, :, :, 0:HALF], src[:, :, :, HALF:ROPE]
                sin = sincos[:, 0, :, :].unsqueeze(2).to_broadcast([P, NT, n, HALF])
                cos = sincos[:, 1, :, :].unsqueeze(2).to_broadcast([P, NT, n, HALF])
                r = [rot[:, m, :, 0:n, :] for m in range(4)]
                tt(r[0], a, cos, ALU.mult)
                tt(r[1], b, sin, ALU.mult)
                tt(r[2], a, sin, ALU.mult)
                link(tt(r[3], b, cos, ALU.mult))
                tt(dst[:, :, :, 0:HALF], r[0], r[1], ALU.subtract)
                return tt(dst[:, :, :, HALF:ROPE], r[2], r[3], ALU.add)

            def angles():
                dve.wait_ge(s_small, 16 * N_SMALL)
                dve.wait_ge(s_const, N_CONST)
                link(nc.vector.tensor_copy(pos_f[:, :], pos_i[:, :]))
                for t in range(NT):
                    for f in range(2):
                        ins = ts(sincos[:, f, t, :], freq[:, :], pos_f[:, t:t + 1], None, ALU.mult)
                link(ins)
                to_int = 1.5 * 2.0 ** 23
                far = 4096.0
                for f, quarter in ((0, 0.0), (1, 0.25)):
                    ins = ts(turns[:, f, :, :], sincos[:, f, :, :], 1.0 / (2.0 * np.pi), quarter, ALU.mult, ALU.add)
                link(ins)
                link(ts(turns[:, :, :, :], turns[:, :, :, :], to_int, to_int, ALU.add, ALU.subtract))
                link(ts(turns_hi[:, :, :, :], turns[:, :, :, :], 1.0 / far, to_int, ALU.mult, ALU.add))
                link(ts(turns_hi[:, :, :, :], turns_hi[:, :, :, :], to_int, far, ALU.subtract, ALU.mult))
                link(tt(turns[:, :, :, :], turns[:, :, :, :], turns_hi[:, :, :, :], ALU.subtract))
                two_pi = 2.0 * np.pi
                c1 = np.floor(two_pi * 2 ** 9) / 2 ** 9
                c2 = np.floor((two_pi - c1) * 2 ** 21) / 2 ** 21
                c3 = two_pi - c1 - c2
                for c in (c1, c2, c3):
                    for n in (turns_hi, turns):
                        flat = [v[:, :, :, :].rearrange("p f t h -> p (f t h)") for v in (sincos, n)]
                        link(stt(out=flat[0], in0=flat[1], scalar=-float(c), in1=flat[0], op0=ALU.mult, op1=ALU.add))
                link(ts(sincos[:, 1, :, :], sincos[:, 1, :, :], float(np.pi / 2), None, ALU.add))
                pi = 3.1415925
                ts(sincos[:, :, :, :], sincos[:, :, :, :], pi, -pi, ALU.min, ALU.max).then_inc(s_angle, 1)

            def step(s):
                kind, a = s[0], s[1:]
                if kind == "x":
                    ps, k = filled(s), 2 * a[0]
                    split_lo(s, [(hT_lo[:, k + n, :], ps[:, n * SEQ:(n + 1) * SEQ], hT_hi[:, k + n, :],
                                  V_ATTN + k + n) for n in range(2)])
                elif kind in ("r1a", "r2a"):
                    src = sumsq if kind == "r1a" else sumsq_x
                    sums(s)
                    link(nc.vector.tensor_reduce(std[:, 0:NT], src[:, :].rearrange("p (t c) -> p t c", t=NT), AX.X,
                                                 ALU.add))
                    mean(NT, D)
                elif kind == "r1b":
                    reciprocal(("r1a",), r_in[:, :], NT)
                elif kind == "r2b":
                    reciprocal(("r2a",), r_ffn[:, :], NT)
                elif kind == "angles":
                    angles()
                elif kind == "lat_a":
                    sums(s)
                    ts(std[:, 0:NT], sumsq[:, 0:NT], 1.0 / LORA, EPS, ALU.mult, ALU.add).then_inc(s_mean, 1)
                elif kind == "lat_in":
                    ps, read = block_banks("lat", a[0])
                    for t in range(NT):
                        for b, c0, n, i, at in LAT_PIECES:
                            if b == a[0]:
                                dst = krw[:, t, :] if i == 2 else latents[i][:, t, at:at + n]
                                ins = ts(dst, ps[t][:, c0:c0 + n], r_in[:, t:t + 1], None, ALU.mult)
                        ins.then_inc(read, 1)
                elif kind == "lat_b":
                    reciprocal(("lat_a",) + a, inv[:, 0:NT], NT)
                    for t in range(NT):
                        v = latents[a[0]][:, t, :]
                        ts(v, v, inv[:, t:t + 1], None, ALU.mult).then_inc(s_lat, 1)
                elif kind == "lat_t":
                    i, j = a
                    ps, k, col = filled(s), 4 * i + 2 * j, (V_KVN if i else V_QN) + 2 * j
                    split_lo(s, [(mT_lo[:, k + n, :], ps[:, n * SEQ:(n + 1) * SEQ], mT_hi[:, k + n, :], col + n)
                                 for n in range(2)])
                elif kind == "kr_b":
                    b = BLOCK_OF[("lat", 2)]
                    dve.wait_ge(s_taken[b % 2], taken(b))
                    link(tt(krw[:, :, :], krw[:, :, :],
                            kw_row[:, NOPE:QK].unsqueeze(1).to_broadcast([P, NT, ROPE]), ALU.mult))
                    dve.wait_ge(s_sin, 1)
                    link(rotate(kr[:, :, :].unsqueeze(2), krw[:, :, :].unsqueeze(2)))
                elif kind == "lb_a":
                    dve.wait_ge(s_lbin, 16 * (a[0] + 1))
                    link(tt(lb_tmp[:, :], lb[:, 0, :], lb[:, 1, :], ALU.max))
                    tt(lb[:, 0, :], lb[:, 0, :], lb_tmp[:, :], ALU.subtract)
                    tt(lb[:, 1, :], lb[:, 1, :], lb_tmp[:, :], ALU.subtract).then_inc(s_lbmax, 1)
                elif kind == "lb_b":
                    dve.wait_ge(s_lbexp, a[0] + 1)
                    link(tt(lb_tmp[:, :], lb[:, 0, :], lb[:, 1, :], ALU.add))
                    link(nc.vector.reciprocal(lb_tmp[:, 0:GW // 2], lb_tmp[:, 0:GW // 2]))
                elif kind == "lb_c":
                    link(nc.vector.reciprocal(lb_tmp[:, GW // 2:], lb_tmp[:, GW // 2:]))
                    link(tt(lb[:, 0, :], lb[:, 0, :], lb_tmp[:, :], ALU.mult))
                    link(ts(lb[:, 1, :], lb[:, 0, :], -1.0, 1.0, ALU.mult, ALU.add))
                    link(ts(lb[:, 0, :], lb[:, 0, :], 1e-19, None, ALU.max))
                elif kind == "q_a":
                    sums(s)
                    ts(std[:, 0:4], sumsq[:, 0:4], 1.0 / QK, EPS, ALU.mult, ALU.add).then_inc(s_mean, 1)
                elif kind == "k_a":
                    sums(s)
                    link(tt(std[:, 0:4].rearrange("p (t h) -> p t h", t=NT),
                            sumsq[:, 0:4].rearrange("p (t h) -> p t h", t=NT),
                            sumsq_kr[:, :].unsqueeze(2).to_broadcast([P, NT, 2]), ALU.add))
                    mean(4, QK)
                elif kind in ("q_b", "k_b"):
                    j, b = a[0], int(kind == "k_b")
                    ps, read = block_banks("uq" if kind == "q_b" else "ukv", j)
                    reciprocal((kind[0] + "_a",) + a, inv[:, 0:4], 4)
                    if j:
                        dve.wait_ge(s_side, USE[(kind[0] + "_t", j - 1, 1)] + 1)
                    if kind == "q_b":
                        for t in range(NT):
                            for h in range(2):
                                ins = stt(out=stage[:, b, t, h, :], in0=ps[t][:, h * QK:(h + 1) * QK],
                                          scalar=inv[:, 2 * t + h:2 * t + h + 1], in1=qw_row[:, :],
                                          op0=ALU.mult, op1=ALU.mult)
                            ins.then_inc(read, 1)
                        dve.wait_ge(read, taken(BLOCK_OF[("uq", j)]))
                        rotate(stage_r[:, b, :, :, :], stage[:, b, :, :, NOPE:QK]).then_inc(s_stage, 1)
                    else:
                        dve.wait_ge(s_val, NT * (j + 1))
                        for t in range(NT):
                            for h in range(2):
                                at = h * (NOPE + P)
                                ins = stt(out=stage[:, b, t, h, 0:NOPE], in0=ps[t][:, at:at + NOPE],
                                          scalar=inv[:, 2 * t + h:2 * t + h + 1], in1=kw_row[:, 0:NOPE],
                                          op0=ALU.mult, op1=ALU.mult)
                            ins.then_inc(read, 1)
                        for t in range(NT):
                            for h in range(2):
                                ins = ts(stage_r[:, b, t, h, :], kr[:, t, :], inv[:, 2 * t + h:2 * t + h + 1], None,
                                         ALU.mult)
                        ins.then_inc(s_stage, 1)
                elif kind == "scores":
                    h, b = a[0], a[0] % 2
                    ps = filled(s)
                    if h >= 2:
                        dve.wait_ge(s_side, USE[("probs_t", h - 2)] + 1)
                    for t, (lo, hi) in enumerate(((0, P), (P, 3 * P))):
                        ins = nc.vector.tensor_tensor_reduce(
                            out=probs[:, b, lo:hi], in0=ps[:, lo:hi], in1=mask_add[:, 2 * P - (hi - lo):2 * P],
                            scale=1.0, scalar=-3.0e38, op0=ALU.add, op1=ALU.max, accum_out=top[:, 2 * b + t:2 * b + t + 1])
                    ins.then_inc(s_given["dve"], 1)
                    dve.wait_ge(s_given["dve"], GIVEN[USE[s]])
                    ts(shift[:, 2 * b:2 * b + 2], top[:, 2 * b:2 * b + 2], -SCALE, None, ALU.mult).then_inc(s_top, 1)
                elif kind == "softmax":
                    h, b = a[0], a[0] % 2
                    dve.wait_ge(s_exp, NT * (h + 1))
                    link(nc.vector.reciprocal(inv_p[:, 2 * b:2 * b + 2], total_p[:, 2 * b:2 * b + 2]))
                    for t, (lo, hi) in enumerate(((0, P), (P, 3 * P))):
                        ins = ts(probs[:, b, lo:hi], probs[:, b, lo:hi], inv_p[:, 2 * b + t:2 * b + t + 1], None,
                                 ALU.mult)
                    ins.then_inc(s_prob, 1)
                elif kind == "attend":
                    split_lo(s, [(mT_lo[:, MT[a[0]], :], filled(s)[:, 0:SEQ], mT_hi[:, MT[a[0]], :], None)])
                elif kind == "hf_a":
                    g = a[0]
                    b = BLOCK_OF[("hf", g)]
                    dve.wait_ge(s_taken[b % 2], taken(b))
                    if g:
                        dve.wait_ge(s_side, USE[("turn", 0, 1, NT - 1)] + 1)
                    wide = [lb[:, n, :].unsqueeze(1).to_broadcast([P, NT, GW]) for n in range(2)]
                    link(tt(hlf[:, :, :], hlf[:, :, :], wide[1], ALU.mult))
                    tt(hlf[:, :, :], hlf[:, :, :], wide[0], ALU.add).then_inc(s_lbused, 1)
                    dve.wait_ge(s_lbused, g + 1)
                    ts(hk[:, :, :], hlf[:, :, :], -1.0, 1.0, ALU.mult, ALU.add).then_inc(s_f, 1)
                elif kind == "lev_a":
                    g, l = a
                    dve.wait_ge(s_given["act"], GIVEN[USE[("turn", g, 2, NT - 1)]])
                    if l > 2:
                        dve.wait_ge(s_side, USE[("pairs", g, l - 2)] + 1)
                    elif g:
                        dve.wait_ge(s_side, USE[("o_t", g - 1, 1)] + 1)
                    h = 1 << (l - 1)
                    n = GH * SEQ // (2 * h)
                    b_ = hbT[:, :, :].rearrange("p a t -> p (a t)").rearrange("p (n w) -> p n w", w=2 * h)
                    mid = b_[:, :, h - 1:h].to_broadcast([P, n, 2 * h])
                    tt(E[:, l % 2, :].rearrange("p (n w) -> p n w", w=2 * h), b_, mid, ALU.subtract)\
                        .then_inc(s_arg, 1)
                elif kind == "lev_b":
                    g, l = a
                    dve.wait_ge(s_dec, (LEVELS + 1) * g + l)
                    e, k_, q_ = [v.rearrange("p (n two h) -> p n two h", two=2, h=1 << (l - 1)) for v in
                                 (E[:, l % 2, :], hkT[:, :, :].rearrange("p a t -> p (a t)"),
                                  hqT[:, :, :].rearrange("p a t -> p (a t)"))]
                    tt(e[:, :, 0, :], e[:, :, 0, :], k_[:, :, 0, :], ALU.mult)
                    tt(e[:, :, 1, :], e[:, :, 1, :], q_[:, :, 1, :], ALU.mult).then_inc(s_lev, 1)
                elif kind == "pairs":
                    g, l = a
                    for t in range(NT):
                        use = s + (t,) if l == 0 else s
                        ps = filled(use)
                        if GIVEN[USE[use]] > 1:
                            dve.wait_ge(s_given["dve"], GIVEN[USE[use]] - 1)
                        if l == 0:
                            ins = nc.vector.copy_predicated(
                                hS[:, :, t, :], ident[:, :].bitcast(I32).unsqueeze(1).to_broadcast([P, GH, P]),
                                ps[:, :].rearrange("p (h t) -> p h t", h=GH))
                            ins.then_inc(s_given["dve"], 1)
                        else:
                            half = 1 << (l - 1)
                            n = P // (2 * half)
                            dst = hS[:, :, t, :].rearrange("p h (n two w) -> p h n two w", two=2, w=half)[:, :, :, 1, :]
                            mask = masks[:, l - 1, :].bitcast(I32)\
                                .rearrange("p (n two w) -> p n two w", two=2, w=half)[:, :, 1, :]
                            ins = nc.vector.copy_predicated(
                                dst, mask.unsqueeze(1).to_broadcast([P, GH, n, half]),
                                ps[:, t * SEQ:(t + 1) * SEQ].rearrange("p (h n w) -> p h n w", h=GH, w=half))
                    if l:
                        ins.then_inc(s_given["dve"], 1)
                elif kind == "join_a":
                    g = a[0]
                    dve.wait_ge(s_side, USE[("pairs", g, LEVELS)] + 1)
                    b_ = hbT[:, :, :].rearrange("p h (c t) -> p (h c) t", t=CHUNK)
                    last = b_[:, :, CHUNK - 1:CHUNK].to_broadcast([P, GH * SEQ // CHUNK, CHUNK])
                    tt(E[:, 0, :].rearrange("p (n t) -> p n t", t=CHUNK), b_, last, ALU.subtract).then_inc(s_arg, 1)
                elif kind == "join_b":
                    g = a[0]
                    dve.wait_ge(s_dec, (LEVELS + 1) * (g + 1))
                    tt(E[:, 0, :], E[:, 0, :], hkT[:, :, :].rearrange("p a t -> p (a t)"), ALU.mult)
                    tt(E[:, 1, :], E[:, 1, :], hqT[:, :, :].rearrange("p a t -> p (a t)"), ALU.mult)\
                        .then_inc(s_lev, 1)
                    dve.wait_ge(s_lev, (LEVELS + 1) * (g + 1))
                elif kind == "join_c":
                    g = a[0]
                    dve.wait_ge(s_side, USE[("join7", g)] + 1)
                    v = E[:, 0, :].rearrange("p (h t) -> p h t", h=GH)[:, :, 0:CHUNK]
                    tt(v, v, chunk_decay[:, :, 1:2].to_broadcast([P, GH, CHUNK]), ALU.mult)
                    v = E[:, 1, :].rearrange("p (h t) -> p h t", h=GH)[:, :, 3 * CHUNK:SEQ]
                    tt(v, v, chunk_decay[:, :, 2:3].to_broadcast([P, GH, CHUNK]), ALU.mult).then_inc(s_join, 1)
                elif kind == "o_a":
                    sums(s)
                    ts(std[:, 0:NT * GH], sumsq[:, 0:NT * GH], 1.0 / P, EPS, ALU.mult, ALU.add).then_inc(s_mean, 1)
                elif kind == "o_b":
                    g = a[0]
                    b = BLOCK_OF[("hg", g)]
                    dve.wait_ge(s_taken[b % 2], taken(b))
                    reciprocal(("o_a", g), inv[:, :], NT * GH)
                    for t in range(NT):
                        ps = bank(USE[("o_a", g, t)])
                        for h in range(GH):
                            cols = slice(h * P, (h + 1) * P)
                            ins = stt(out=E[:, 0, t * GW:(t + 1) * GW][:, cols], in0=ps[:, cols],
                                      scalar=inv[:, GH * t + h:GH * t + h + 1], in1=hgate[:, t, cols],
                                      op0=ALU.mult, op1=ALU.mult)
                        ins.then_inc(s_given["dve"], 1)
                elif kind == "o_t":
                    g, j = a
                    hi, lo, k = (hT_hi, hT_lo, 12 + 2 * j) if g else (mT_hi, mT_lo, MT[HEADS + 2 * j])
                    split_lo(s, [(lo[:, k:k + 2, :], filled(s)[:, :].rearrange("p (k t) -> p k t", k=2),
                                  hi[:, k:k + 2, :], V_HG)])
                elif kind in ("out1", "out2"):
                    c = a[0]
                    ps, read = block_banks(kind, c)
                    if kind == "out1":
                        dve.wait_ge(s_xagain, 16)
                    else:
                        b = BLOCK_OF[("out1", c)]
                        dve.wait_ge(s_taken[b % 2], taken(b))
                    for t in range(NT):
                        v = X[:, t, c * NB:(c + 1) * NB]
                        tt(v, v, ps[t][:, :], ALU.add).then_inc(read, 1)
                elif kind == "x2":
                    ps, k = filled(s), 4 * a[0] + 2 * a[1]
                    split_lo(s, [(hT_lo[:, k + n, :], ps[:, n * SEQ:(n + 1) * SEQ], hT_hi[:, k + n, :],
                                  V_FFN + k + n) for n in range(2)])

            def multiply_gate(i):
                dve.wait_ge(s_used, G0 + GU + GU * i)
                dve.wait_ge(s_taken[PG], taken(FF) + NT * i)
                for t in range(NT):
                    stt(out=hidden[:, t, :], in0=main[PU][t][:, :], scalar=r_ffn[:, t:t + 1], in1=gate[:, t, :],
                        op0=ALU.mult, op1=ALU.mult).then_inc(s_taken[PU], 1)

            def split_hidden(i):
                for u in range(2):
                    dve.wait_ge(s_ahi, 2 * i + u + 1)
                    at = bass.ds(4 * i + 2 * u, 2)
                    tt(aT_lo[:, at, :], side[u][:, :].rearrange("p (k t) -> p k t", k=2),
                       aT_hi[:, at, :].bitcast(F32), ALU.subtract).then_inc(s_alo, 1)

            def add_down(d):
                b = DOWN + d
                dve.wait_ge(s_used, G1 + DN * (d + 1))
                for t in range(NT):
                    v = X[:, t, d * NB:(d + 1) * NB]
                    tt(v, v, main[b % 2][t][:, :], ALU.add).then_inc(s_taken[b % 2], 1)

            for g in range(FIRST, G0):
                n = g + LEAD
                if n >= 0:
                    convert(n % RING, n, granule_size(n))
                for s in steps_at(g):
                    step(s)
            for j in range(GU):
                n = G0 + j + LEAD
                convert(n % RING, n)
                for s in steps_at(G0 + j):
                    step(s)
            with dve.Fori(1, NFF) as i:
                for j in range(GU):
                    n = G0 + j + LEAD
                    convert(n % RING, n + GU * i)
                    if j == 0:
                        multiply_gate(i - 1)
                    if j == 3:
                        split_hidden(i - 1)
            multiply_gate(NFF - 1)
            split_hidden(NFF - 1)
            for j in range(4 * DN):
                n = G1 + j + LEAD
                if n < G1 + 4 * DN:
                    convert(n % RING, n)
                if j and j % DN == 0:
                    add_down(j // DN - 1)
            add_down(3)

        @block.tensor
        def _(pe):
            matmul, transpose = nc.tensor.matmul, nc.tensor.transpose

            def multiply(slot, g, lhs, k_first, k_last, banks, cols, ks):
                hi, lo, at = lhs
                pe.wait_ge(s_lo, g + 1)
                for part in ("hi", "lo"):
                    w = w_hi if part == "hi" else w_lo
                    for n, k in enumerate(ks):
                        rhs = w[:, slot, n * cols:(n + 1) * cols]
                        for t in range(NT):
                            tok = slice(t * P, (t + 1) * P)
                            m = matmul(banks[t][:, 0:cols], hi[:, at[n], tok], rhs,
                                       start=(part == "hi" and k == k_first), stop=(part == "lo" and k == k_last))
                            if part == "hi":
                                matmul(banks[t][:, 0:cols], lo[:, at[n], tok], rhs, start=False, stop=False)
                m.then_inc(s_used, 1)

            def use(key):
                n = USE[key]
                if n >= SIDE:
                    pe.wait_ge(s_given[USES[n - SIDE][1]], GIVEN[n - SIDE])
                return bank(n)

            def given(key):
                pe.wait_ge(s_given["act"], GIVEN[USE[key]])

            def turn_x(s, k, where=X):
                ps = use(s)
                for n in range(2):
                    for t in range(NT):
                        at = n * SEQ + t * P
                        m = transpose(ps[:, at:at + P], where[:, t, (k + n) * P:(k + n + 1) * P], ident[:, :])
                m.then_inc(s_side, 1)

            def step(s):
                kind, a = s[0], s[1:]
                if kind == "vec":
                    if a[0]:
                        pe.wait_ge(s_small, 16 * N_SMALL)
                        src = more_rows
                    else:
                        pe.wait_ge(s_attn, 16)
                        pe.wait_ge(s_const, N_IDENT)
                        src = vec_rows
                    n = src.shape[0]
                    transpose(use(s)[:, 0:n], src[:, :], ident[0:n, 0:n]).then_inc(s_side, 1)
                elif kind == "x":
                    pe.wait_ge(s_x[a[0]], 16)
                    turn_x(s, 2 * a[0])
                elif kind == "x2":
                    c, j = a
                    b = BLOCK_OF[("out2", c)]
                    pe.wait_ge(s_taken[b % 2], taken(b))
                    turn_x(s, 4 * c + 2 * j)
                elif kind == "lat_t":
                    i, j = a
                    pe.wait_ge(s_lat, NT * (i + 1))
                    turn_x(s, 2 * j, latents[i])
                elif kind in ("q_t", "k_t"):
                    j, b = a[0], int(kind == "k_t")
                    pe.wait_ge(s_stage, 2 * j + b + 1)
                    ps = use(s + (0,))
                    for h in range(2):
                        for t in range(NT):
                            at = h * SEQ + t * P
                            m = transpose(ps[:, at:at + P], stage[:, b, t, h, 0:NOPE], ident[:, :])
                    m.then_inc(s_side, 1)
                    ps = use(s + (1,))
                    for t in range(NT):
                        m = transpose(ps[:, t * P:(t + 1) * P], stage_r[:, b, t, :, :].rearrange("p h r -> p (h r)"),
                                      ident[:, :])
                    m.then_inc(s_side, 1)
                elif kind == "scores":
                    h = a[0]
                    given(("k_t", h // 2, 1))
                    ps = use(s)
                    part = slice((h % 2) * ROPE, (h % 2 + 1) * ROPE)
                    for t, keys, cols in ((0, slice(0, P), slice(0, P)), (1, slice(0, SEQ), slice(P, 3 * P))):
                        tok = slice(t * P, (t + 1) * P)
                        matmul(ps[:, cols], qTn[:, h, tok], kTn[:, h, keys], start=True, stop=False)
                        m = matmul(ps[:, cols], qTr[part, h // 2, tok], kTr[part, h // 2, keys], start=False, stop=True)
                    m.then_inc(s_side, 1)
                elif kind == "probs_t":
                    h = a[0]
                    pe.wait_ge(s_prob, h + 1)
                    ps = use(s)
                    for n in range(3):
                        cols = slice(n * P, (n + 1) * P)
                        m = transpose(ps[:, cols], probs[:, h % 2, cols], ident[:, :])
                    m.then_inc(s_side, 1)
                elif kind == "attend":
                    h, b = a[0], a[0] % 2
                    given(("probs_t", h))
                    ps = use(s)
                    matmul(ps[:, 0:P], val[:, 0, h, :], probsT[:, b, 0:P], start=True, stop=True)
                    matmul(ps[:, P:SEQ], val[:, 0, h, :], probsT[:, b, P:2 * P], start=True, stop=False)
                    matmul(ps[:, P:SEQ], val[:, 1, h, :], probsT[:, b, 2 * P:3 * P], start=False, stop=True)\
                        .then_inc(s_side, 1)
                elif kind == "turn":
                    g, n, t = a
                    if n == 0:
                        b = BLOCK_OF[("hq", g)]
                        pe.wait_ge(s_taken[b % 2], taken(b))
                    else:
                        pe.wait_ge(s_f if n == 1 else s_logf, g + 1)
                    ps = use(s)
                    for h in range(GH):
                        cols = slice(h * P, (h + 1) * P)
                        if n == 2:
                            m = matmul(ps[:, cols], hlf[:, t, cols], tri[:, :], start=True, stop=True)
                        else:
                            m = transpose(ps[:, cols], (hq, hk)[n][:, t, cols], ident[:, :])
                    m.then_inc(s_side, 1)
                elif kind == "pairs":
                    g, l = a
                    if l == 0:
                        given(("turn", g, 1, NT - 1))
                        for t in range(NT):
                            tok = slice(t * P, (t + 1) * P)
                            ps = use(s + (t,))
                            for h in range(GH):
                                m = matmul(ps[:, h * P:(h + 1) * P], hkT[:, h, tok], hqT[:, h, tok], start=True,
                                           stop=True)
                            m.then_inc(s_side, 1)
                    else:
                        pe.wait_ge(s_lev, (LEVELS + 1) * g + l)
                        ps = use(s)
                        both = E[:, l % 2, :].rearrange("p (h t) -> p h t", h=GH)
                        right = E[:, l % 2, :].rearrange("p (n two w) -> p n two w", two=2, w=1 << (l - 1))
                        n = P >> l
                        for t in range(NT):
                            for h in range(GH):
                                at = (t * GH + h) * P // 2
                                m = matmul(ps[:, at:at + P // 2], both[:, h, t * P:(t + 1) * P],
                                           right[:, (h * NT + t) * n:(h * NT + t + 1) * n, 1, :], start=True, stop=True)
                        m.then_inc(s_side, 1)
                elif kind in ("join7", "join8"):
                    g = a[0]
                    ps = use(s)
                    keys, queries = [E[:, n, :].rearrange("p (h t) -> p h t", h=GH) for n in range(2)]
                    if kind == "join7":
                        pe.wait_ge(s_lev, (LEVELS + 1) * (g + 1))
                        for h in range(GH):
                            for t in range(NT):
                                at = (2 * h + t) * CHUNK
                                m = matmul(ps[0:CHUNK, at:at + CHUNK], keys[:, h, t * P:t * P + CHUNK],
                                           queries[:, h, t * P + CHUNK:(t + 1) * P], start=True, stop=True)
                    else:
                        pe.wait_ge(s_join, g + 1)
                        for h in range(GH):
                            m = matmul(ps[:, h * P:(h + 1) * P], keys[:, h, 0:P], queries[:, h, P:SEQ], start=True,
                                       stop=True)
                    m.then_inc(s_side, 1)
                elif kind == "o_a":
                    g = a[0]
                    b = BLOCK_OF[("hi", g)]
                    pe.wait_ge(s_taken[b % 2], taken(b))
                    pe.wait_ge(s_given["dve"], GIVEN[USE[("pairs", g, LEVELS)]])
                    given(("join8", g))
                    for t in range(NT):
                        ps = use(s + (t,))
                        for h in range(GH):
                            cols = slice(h * P, (h + 1) * P)
                            if t:
                                matmul(ps[:, cols], hS[:, h, 2, :], hv[:, 0, cols], start=True, stop=False)
                            m = matmul(ps[:, cols], hS[:, h, t, :], hv[:, t, cols], start=(t == 0), stop=True)
                        m.then_inc(s_side, 1)
                elif kind == "o_t":
                    g, j = a
                    pe.wait_ge(s_given["dve"], GIVEN[USE[("o_a", g, NT - 1)]])
                    turn_x(s, 2 * j, E[:, 0, :].rearrange("p (t c) -> p t c", t=NT))

            def lhs_of(kind, ks):
                if kind == "ukv":
                    return mT_hi, mT_lo, [4 + k for k in ks]
                if kind == "out1":
                    return mT_hi, mT_lo, [MT[k] for k in ks]
                if kind == "out2":
                    return hT_hi, hT_lo, [12 + k for k in ks]
                return (mT_hi, mT_lo, ks) if kind == "uq" else (hT_hi, hT_lo, ks)

            for g in range(FIRST, 0):
                for s in steps_at(g):
                    step(s)
            for g, (b, k, n) in enumerate(GRANULES):
                for s in steps_at(g):
                    step(s)
                kind, i, _, _, cols, rows, _ = BLOCKS[b]
                ks = list(range(k, k + n))
                pe.wait_ge(s_tlo, split_needed(g))
                if k == 0 and b >= 2:
                    pe.wait_ge(s_taken[b % 2], taken(b - 2))
                multiply(g % RING, g, lhs_of(kind, ks), 0, len(rows) - 1, main[b % 2], cols, ks)

            def turn_hidden(i):
                for t in range(NT):
                    pe.wait_ge(s_taken[PU], taken(FF + 1) - NT + t + 1 + NT * i)
                    for u in range(2):
                        for n in range(2):
                            at = n * SEQ + t * P
                            m = transpose(side[u][:, at:at + P], hidden[:, t, (2 * u + n) * P:(2 * u + n + 1) * P],
                                          ident[:, :])
                        if t == NT - 1:
                            m.then_inc(s_turned, 1)

            def gate_and_up(i, first=False):
                for j in range(GU):
                    g = G0 + j
                    if first:
                        for s in steps_at(g):
                            step(s)
                        pe.wait_ge(s_tlo, SPLIT[("x2",) + divmod(min(j, 7), 2)] + 1)
                    elif j == 3:
                        turn_hidden(i - 1)
                    up = j // (KT // 2)
                    k = 2 * (j % (KT // 2))
                    if k == 0:
                        pe.wait_ge(s_taken[(PG, PU)[up]], taken(FF + up - 2) + NT * i)
                    multiply(g % RING, g + GU * i, (hT_hi, hT_lo, [k, k + 1]), 0, KT - 1, main[(PG, PU)[up]], NB,
                             [k, k + 1])

            gate_and_up(0, True)
            with pe.Fori(1, NFF) as i:
                gate_and_up(i)
            turn_hidden(NFF - 1)
            with pe.Fori(0, 2) as i:
                for j in range(2 * DN):
                    d, k = divmod(j, DN)
                    b = DOWN + d
                    if k == 0:
                        pe.wait_ge(s_taken[b % 2], taken(b - 2) + NT * i)
                    if j == DN - 2:
                        pe.wait_ge(s_alo, 2 * NFF)
                    multiply((G1 + j) % RING, G1 + j + 2 * DN * i, (aT_hi, aT_lo, [2 * k, 2 * k + 1]), 0, DOWN_KT - 1,
                             main[b % 2], NB, [2 * k, 2 * k + 1])


def granule_size(g):
    if g >= G0:
        return GRAN
    b, _, n = GRANULES[g]
    return n * BLOCKS[b][4]


_INS = ["x", "positions", "attn_norm_w", "w_in", "hgrn_lb", "hgrn_norm_w", "mla_q_norm_w", "w_uq", "mla_kv_norm_w",
        "w_ukv", "q_head_norm_w", "k_head_norm_w", "w_out", "ffn_norm_w", "w_gate_up", "w_down"]


def kernel(**inputs):
    import concourse.bacc as bacc
    from concourse.bass_utils import run_bass_kernel_spmd

    nc = bacc.Bacc("TRN2", target_bir_lowering=False, num_devices=1)
    arrays, args = {}, []
    for name in _INS:
        a = np.ascontiguousarray(inputs[name])
        arrays[f"in_{name}"] = a
        args.append(nc.dram_tensor(f"in_{name}", a.shape, mybir.dt.from_np(a.dtype), kind="ExternalInput").ap())
    args.append(nc.dram_tensor("out_0", (1, SEQ, D), F32, kind="ExternalOutput").ap())
    hybrid_layer(nc, *args)
    r = run_bass_kernel_spmd(nc, [arrays], core_ids=[0])
    return r.results[0]["out_0"]
```
